# Optimizing a Trainium2 kernel written in Bass

```python
import jax, jax.numpy as jnp
from jax import lax
import numpy as np

D_MODEL = 1024
BATCH = 1
SEQ = 512
DEPTH = 1

CTX_LEN = 256
GRID_W = 64
HG_HEADS = 8
HG_DK = 128
HG_DV = 128
HG_WK = HG_HEADS * HG_DK
HG_WV = HG_HEADS * HG_DV
HG_CHUNK = 32
RT_HEADS = 8
RT_DK = D_MODEL // RT_HEADS
RT_DV = 2 * D_MODEL // RT_HEADS
RT_WK = RT_HEADS * RT_DK
RT_WV = RT_HEADS * RT_DV
RT_CHUNK = 64
ROPE_BASE = 10000.0
D_FF = ((8 * D_MODEL // 3 + 255) // 256) * 256
EPS = 1e-6
GN_EPS = 1e-5
_SPLIT_SIZES = (HG_WK, HG_WK, HG_WK, HG_WV, HG_WV, RT_WK, RT_WK, RT_WV, RT_WV, D_MODEL, D_MODEL)
D_IN = sum(_SPLIT_SIZES)
_SPLIT_POINTS = tuple(int(v) for v in np.cumsum(_SPLIT_SIZES)[:-1])

kernel_name = "hybrid_hgrn2_retention_dit_block"

def _rmsnorm(x, w):
    xf = x.astype(jnp.float32)
    y = xf * lax.rsqrt(jnp.mean(xf * xf, axis=-1, keepdims=True) + EPS)
    return (y * w.astype(jnp.float32)).astype(x.dtype)

def _modulate(h, shift, scale):
    return h * (1.0 + scale) + shift

def _heads(t, n_heads):
    B, L, _ = t.shape
    return t.reshape(B, L, n_heads, -1).transpose(0, 2, 1, 3)

def _merge_heads(t):
    B, n, L, d = t.shape
    return t.transpose(0, 2, 1, 3).reshape(B, L, n * d)

def _chunk(t, C):
    B, H, L, d = t.shape
    return jnp.moveaxis(t.reshape(B, H, L // C, C, d), 2, 0)

def _unchunk(t):
    n, B, H, C, d = t.shape
    return jnp.moveaxis(t, 0, 2).reshape(B, H, n * C, d)

def _flip(t):
    return jnp.flip(t, axis=2)

def _axial_rope(L):
    rows = L // GRID_W
    row = jnp.repeat(jnp.arange(rows, dtype=jnp.float32), GRID_W)
    col = jnp.tile(jnp.arange(GRID_W, dtype=jnp.float32), rows)
    n_f = RT_DK // 4
    freqs = ROPE_BASE ** (-jnp.arange(n_f, dtype=jnp.float32) / n_f)
    ang = jnp.concatenate([row[:, None] * freqs, col[:, None] * freqs], axis=-1)
    return jnp.cos(ang), jnp.sin(ang)

def _apply_rope(t, cos, sin):
    half = t.shape[-1] // 2
    t1, t2 = t[..., :half], t[..., half:]
    return jnp.concatenate([t1 * cos - t2 * sin, t1 * sin + t2 * cos], axis=-1)

def _hgrn2_scan(q, k, v, lf, s0):
    C = HG_CHUNK
    causal = jnp.tril(jnp.ones((C, C), dtype=bool))[:, :, None]

    def step(s, blk):
        qc, kc, vc, lfc = blk
        b = jnp.cumsum(lfc, axis=2)
        rel = jnp.where(causal, b[:, :, :, None, :] - b[:, :, None, :, :], -jnp.inf)
        att = jnp.sum(qc[:, :, :, None, :] * kc[:, :, None, :, :] * jnp.exp(rel), axis=-1)
        o = (jnp.einsum('bhts,bhse->bhte', att, vc)
             + jnp.einsum('bhtd,bhde->bhte', qc * jnp.exp(b), s))
        b_last = b[:, :, -1:, :]
        s = (jnp.exp(b_last[:, :, 0, :])[..., None] * s
             + jnp.einsum('bhsd,bhse->bhde', kc * jnp.exp(b_last - b), vc))
        return s, o

    _, o = lax.scan(step, s0, (_chunk(q, C), _chunk(k, C), _chunk(v, C), _chunk(lf, C)))
    return _unchunk(o)

def _hgrn2_final_state(k, v, lf):
    b = jnp.cumsum(lf, axis=2)
    return jnp.einsum('bhsd,bhse->bhde', k * jnp.exp(b[:, :, -1:, :] - b), v)

def _retention_scan(q, k, v, log_gamma, s0):
    C = RT_CHUNK
    idx = jnp.arange(C, dtype=jnp.float32)
    diff = idx[:, None] - idx[None, :]
    lg = log_gamma[:, None, None]
    dmat = jnp.where(diff >= 0, jnp.exp(lg * jnp.maximum(diff, 0.0)), 0.0)
    q_decay = jnp.exp(log_gamma[:, None] * (idx + 1.0))[None, :, :, None]
    k_decay = jnp.exp(log_gamma[:, None] * (C - 1.0 - idx))[None, :, :, None]
    s_decay = jnp.exp(log_gamma * C)[None, :, None, None]

    def step(s, blk):
        qc, kc, vc = blk
        att = jnp.einsum('bhtd,bhsd->bhts', qc, kc) * dmat
        o = (jnp.einsum('bhts,bhse->bhte', att, vc)
             + jnp.einsum('bhtd,bhde->bhte', qc * q_decay, s))
        s = s_decay * s + jnp.einsum('bhsd,bhse->bhde', kc * k_decay, vc)
        return s, o

    _, o = lax.scan(step, s0, (_chunk(q, C), _chunk(k, C), _chunk(v, C)))
    return _unchunk(o)

def _retention_final_state(k, v, log_gamma):
    L = k.shape[2]
    w = jnp.exp(log_gamma[:, None] * (L - 1.0 - jnp.arange(L, dtype=jnp.float32)))
    return jnp.einsum('bhsd,hs,bhse->bhde', k, w, v)

def _head_rms(t):
    return t * lax.rsqrt(jnp.mean(t * t, axis=-1, keepdims=True) + EPS)

def _group_norm(t):
    mu = jnp.mean(t, axis=-1, keepdims=True)
    var = jnp.mean(jnp.square(t - mu), axis=-1, keepdims=True)
    return (t - mu) * lax.rsqrt(var + GN_EPS)

def _mixer_inputs(h, w_in, lb_f, lb_b, rope):
    p = jnp.matmul(h, w_in).astype(jnp.float32)
    hq, hf_f, hf_b, hi, hg, rq, rk, rv, rg, ga, gb = jnp.split(p, _SPLIT_POINTS, axis=-1)

    def forget(z, lb):
        k = _heads((1.0 - lb) * jax.nn.sigmoid(-z), HG_HEADS)
        lf = _heads(jnp.log(lb + (1.0 - lb) * jax.nn.sigmoid(z)), HG_HEADS)
        return k, lf

    hk_f, hlf_f = forget(hf_f, lb_f)
    hk_b, hlf_b = forget(hf_b, lb_b)
    rq = _heads(rq, RT_HEADS) * RT_DK ** -0.5
    rk = _heads(rk, RT_HEADS)
    if rope is not None:
        rq = _apply_rope(rq, rope[0], rope[1])
        rk = _apply_rope(rk, rope[0], rope[1])
    return dict(hq=_heads(hq, HG_HEADS) * HG_DK ** -0.5, hk_f=hk_f, hlf_f=hlf_f,
                hk_b=hk_b, hlf_b=hlf_b, hv=_heads(hi, HG_HEADS), hg=hg,
                rq=rq, rk=rk, rv=_heads(rv, RT_HEADS), rg=rg, ga=ga, gb=gb)

def _context_states(p, log_g_f, log_g_b):
    s_hf = _hgrn2_final_state(p["hk_f"], p["hv"], p["hlf_f"])
    s_hb = _hgrn2_final_state(_flip(p["hk_b"]), _flip(p["hv"]), _flip(p["hlf_b"]))
    s_rf = _retention_final_state(p["rk"], p["rv"], log_g_f)
    s_rb = _retention_final_state(_flip(p["rk"]), _flip(p["rv"]), log_g_b)
    return s_hf, s_hb, s_rf, s_rb

def _mix(p, s_hf, s_hb, s_rf, s_rb, log_g_f, log_g_b, hg_norm_w, w_pa, w_pb, w_out):
    hg = (_hgrn2_scan(p["hq"], p["hk_f"], p["hv"], p["hlf_f"], s_hf)
          + _flip(_hgrn2_scan(_flip(p["hq"]), _flip(p["hk_b"]), _flip(p["hv"]),
                              _flip(p["hlf_b"]), s_hb)))
    rt = (_retention_scan(p["rq"], p["rk"], p["rv"], log_g_f, s_rf)
          + _flip(_retention_scan(_flip(p["rq"]), _flip(p["rk"]), _flip(p["rv"]), log_g_b, s_rb)))
    ya = _merge_heads(_head_rms(hg)) * hg_norm_w * jax.nn.silu(p["hg"])
    yb = _merge_heads(_group_norm(rt)) * jax.nn.silu(p["rg"])
    merged = (jax.nn.sigmoid(p["ga"]) * jnp.matmul(ya, w_pa)
              + jax.nn.sigmoid(p["gb"]) * jnp.matmul(yb, w_pb))
    return jnp.matmul(merged, w_out)

def _swiglu(h, w_gate, w_up, w_down):
    return jnp.matmul(jax.nn.silu(jnp.matmul(h, w_gate)) * jnp.matmul(h, w_up), w_down)

def setup_inputs(seed: int = 0) -> dict:
    key = jax.random.key(seed)
    ks = jax.random.split(key, 24)
    f32 = jnp.float32

    def nrm(k, shape, scale):
        return jax.random.normal(k, shape, f32) * scale

    gamma = 1.0 - 2.0 ** (-5.0 - jnp.arange(RT_HEADS, dtype=f32))
    theta0 = jnp.log(gamma) - jnp.log1p(-gamma)
    return {
        "x": nrm(ks[0], (BATCH, SEQ, D_MODEL), 1.0),
        "c": nrm(ks[1], (BATCH, D_MODEL), 1.0),
        "ctx": nrm(ks[2], (BATCH, CTX_LEN, D_MODEL), 1.0),
        "c_ctx": nrm(ks[3], (D_MODEL,), 1.0),
        "w_mod": nrm(ks[4], (DEPTH, D_MODEL, 6 * D_MODEL), 0.5 * D_MODEL ** -0.5),
        "b_mod": nrm(ks[5], (DEPTH, 6 * D_MODEL), 0.02),
        "norm1_w": 1.0 + nrm(ks[6], (DEPTH, D_MODEL), 0.02),
        "norm2_w": 1.0 + nrm(ks[7], (DEPTH, D_MODEL), 0.02),
        "w_in": nrm(ks[8], (DEPTH, D_MODEL, D_IN), D_MODEL ** -0.5),
        "hg_lb_fwd": nrm(ks[9], (DEPTH + 1, HG_WK), 0.1),
        "hg_lb_bwd": nrm(ks[10], (DEPTH + 1, HG_WK), 0.1),
        "hg_norm_w": 1.0 + nrm(ks[11], (DEPTH, HG_WV), 0.02),
        "rt_theta_fwd": theta0 + nrm(ks[12], (DEPTH, RT_HEADS), 0.1),
        "rt_theta_bwd": theta0 + nrm(ks[13], (DEPTH, RT_HEADS), 0.1),
        "w_proj_hgrn": nrm(ks[14], (DEPTH, HG_WV, D_MODEL), HG_WV ** -0.5),
        "w_proj_ret": nrm(ks[15], (DEPTH, RT_WV, D_MODEL), RT_WV ** -0.5),
        "w_out": nrm(ks[16], (DEPTH, D_MODEL, D_MODEL), D_MODEL ** -0.5),
        "w_ffn_gate": nrm(ks[17], (DEPTH, D_MODEL, D_FF), D_MODEL ** -0.5),
        "w_ffn_up": nrm(ks[18], (DEPTH, D_MODEL, D_FF), D_MODEL ** -0.5),
        "w_ffn_down": nrm(ks[19], (DEPTH, D_FF, D_MODEL), D_FF ** -0.5),
        "final_norm_w": 1.0 + nrm(ks[20], (D_MODEL,), 0.02),
    }

def reference(x, c, ctx, c_ctx, w_mod, b_mod, norm1_w, norm2_w, w_in, hg_lb_fwd, hg_lb_bwd,
              hg_norm_w, rt_theta_fwd, rt_theta_bwd, w_proj_hgrn, w_proj_ret, w_out,
              w_ffn_gate, w_ffn_up, w_ffn_down, final_norm_w):
    B, L, _ = x.shape
    f32 = jnp.float32
    rope = _axial_rope(L)
    lb_f_all = jnp.cumsum(jax.nn.softmax(hg_lb_fwd.astype(f32), axis=0), axis=0)
    lb_b_all = jnp.cumsum(jax.nn.softmax(hg_lb_bwd.astype(f32), axis=0), axis=0)
    hg_zero = jnp.zeros((B, HG_HEADS, HG_DK, HG_DV), f32)
    rt_zero = jnp.zeros((B, RT_HEADS, RT_DK, RT_DV), f32)

    for l in range(DEPTH):
        last = l == DEPTH - 1
        mod_x = (jnp.matmul(jax.nn.silu(c), w_mod[l]) + b_mod[l])[:, None, :]
        mod_c = jnp.matmul(jax.nn.silu(c_ctx), w_mod[l]) + b_mod[l]
        sh1, sc1, g1, sh2, sc2, g2 = jnp.split(mod_x, 6, axis=-1)
        sh1c, sc1c, g1c, sh2c, sc2c, g2c = jnp.split(mod_c, 6, axis=-1)
        log_g_f = jax.nn.log_sigmoid(rt_theta_fwd[l].astype(f32))
        log_g_b = jax.nn.log_sigmoid(rt_theta_bwd[l].astype(f32))
        branch_w = (hg_norm_w[l], w_proj_hgrn[l], w_proj_ret[l], w_out[l])

        hc = _modulate(_rmsnorm(ctx, norm1_w[l]), sh1c, sc1c)
        pc = _mixer_inputs(hc, w_in[l], lb_f_all[l], lb_b_all[l], None)
        s_hf, s_hb, s_rf, s_rb = _context_states(pc, log_g_f, log_g_b)
        if not last:
            ctx_mix = _mix(pc, hg_zero, hg_zero, rt_zero, rt_zero, log_g_f, log_g_b, *branch_w)
            ctx = ctx + g1c * ctx_mix.astype(ctx.dtype)
            hc2 = _modulate(_rmsnorm(ctx, norm2_w[l]), sh2c, sc2c)
            ctx = ctx + g2c * _swiglu(hc2, w_ffn_gate[l], w_ffn_up[l], w_ffn_down[l])

        hx = _modulate(_rmsnorm(x, norm1_w[l]), sh1, sc1)
        px = _mixer_inputs(hx, w_in[l], lb_f_all[l], lb_b_all[l], rope)
        x_mix = _mix(px, s_hf, s_hb, s_rf, s_rb, log_g_f, log_g_b, *branch_w)
        x = x + g1 * x_mix.astype(x.dtype)
        hx2 = _modulate(_rmsnorm(x, norm2_w[l]), sh2, sc2)
        x = x + g2 * _swiglu(hx2, w_ffn_gate[l], w_ffn_up[l], w_ffn_down[l])

    return _rmsnorm(x, final_norm_w)


_drawn_inputs = setup_inputs


def setup_inputs(seed=0):
    import zlib

    import numpy as np

    out = dict(_drawn_inputs(seed))
    spreads = {}
    factors = {'norm1_w': 8.0,
     'norm2_w': 8.0,
     'hg_lb_fwd': 8.0,
     'hg_lb_bwd': 8.0,
     'hg_norm_w': 8.0,
     'final_norm_w': 2.949}
    for name, (base, spread) in spreads.items():
        noise = np.random.default_rng([zlib.crc32(name.encode()), seed]).standard_normal(out[name].shape)
        drawn = base * np.exp(spread * noise) if base else spread * noise
        out[name] = __import__('jax').numpy.asarray(drawn.astype(out[name].dtype))
    for name, factor in factors.items():
        out[name] = (out[name] * factor).astype(out[name].dtype)
    return out
```

```python
from contextlib import ExitStack

import numpy as np
import concourse.bass as bass
from concourse import mybir

F32 = mybir.dt.float32
F32R = mybir.dt.float32r
F16 = mybir.dt.float16
U8 = mybir.dt.uint8
ACT = mybir.ActivationFunctionType
ALU = mybir.AluOpType

P = 128
D = 1024
KT = D // P
L = 512
LC = 256
NT, NC = L // P, LC // P
H = 8
DK = 128
GRID_W = 64
D_FF = 2816
FT = D_FF // P
EPS, GN_EPS = 1e-6, 1e-5
QSCALE = DK ** -0.5

COL = dict(hq=0, hf_f=1024, hf_b=2048, hi=3072, hg=4096, rq=5120, rk=6144, rv=7168, rg=9216, ga=11264, gb=12288)

PC, PCC, PN1, PN2, PFN, PHG, PLF, PLB, PBM = 0, 8, 16, 24, 32, 40, 48, 64, 80
LBF, OMF, LBB, OMB, HGN, LGF, LGB, WC = 0, 1, 2, 3, 4, 5, 6, 7
HPN = 11

SLABS = [
    ("rg0", COL["rg"], 256, 0, False), ("rg1", COL["rg"], 256, 1, False), ("g", COL["hg"], 128, 0, False),
    ("f", COL["hf_f"], 128, 0, True), ("b", COL["hf_b"], 128, 0, True), ("q", COL["hq"], 128, 0, False),
    ("v", COL["hi"], 128, 0, True), ("rk", COL["rk"], 128, 0, True), ("rv0", COL["rv"], 256, 0, True),
    ("rv1", COL["rv"], 256, 1, True), ("rq", COL["rq"], 128, 0, False),
]
GEMM = {s[0]: i for i, s in enumerate(SLABS)}
NSLAB = len(SLABS) + 3
HALVES = [64, 32, 16, 8, 4, 2, 1]
STEPS = [
    "rg0.a", "rg0.b", "rg0.d", "mod0", "rg1.a", "rg1.b", "rg1.d", "mod1", "g.a", "g.b", "g.d", "mod2",
    "f.a", "f.b", "f.d", "f.c", "f.e", "b.a", "b.b", "b.d", "b.c", "b.e", "gates",
    "q.a", "strip", "q.b", "q.d", "mod3", "v.a", "v.b", "v.d", "v.c", "v.e", "prep0",
    "rk.a", "Tv", "prep1", "mul0", "rk.b", "rk.d", "job0", "prep2", "mul1", "rk.c", "rk.e",
    "job1", "rv0.a", "KVc", "prep3", "mul2", "post1", "rv0.b", "rv0.d", "job2", "prep4", "mul3", "post2", "rv0.c", "rv0.e",
    "job3", "Trv0", "prep5", "mul4", "post3", "rv1.a", "job4", "prep6", "mul5", "post4", "rv1.b", "rv1.d",
    "job5", "prep7", "mul6", "post5", "rv1.c", "rv1.e", "job6", "Trv1", "mul7",
    "rq.a", "job7", "mul8", "post6", "prep9", "post7", "rq.b", "rq.d", "job8", "prep10", "mul9", "post8",
    "job9", "rkT", "mul10", "job10", "KVf", "rKV", "prep11", "mul11", "att0", "att1", "KVb", "av0", "att2", "av1", "att3", "av2",
    "hgo", "av3", "hstat", "rstate", "rmean", "hnorm", "rvar", "pa", "rnorm", "pb",
]

MIX = ["Tv", "Tvc", "job0", "job1", "KVc", "job2", "job3", "Trv0", "Trv0c", "job4", "job5", "job6",
       "Trv1", "Trv1c", "job7", "job8", "job9", "rkT", "job10", "KVf", "rKV", "att0", "att1", "KVb", "att2",
       "att3", "hstat", "rmean", "rvar"]
CTXU = ["mod0", "mod1", "mod2", "f", "b", "mod3", "v", "rk", "rv0", "rv1"]


def bank_uses():
    where, count = {}, {}

    def put(name, bank):
        where[name] = (bank, count.get(bank, 0))
        count[bank] = count.get(bank, 0) + 1

    for i, s in enumerate(SLABS):
        put(s[0], i % 2)
    for n in range(8):
        put(f"pa{n}", (len(SLABS) + n) % 2)
    for n in range(8):
        put(f"pb{n}", (len(SLABS) + 8 + n) % 2)
    for u in CTXU:
        put(u + ".ctx", 2)
    for i, u in enumerate(MIX):
        put(u, 3 + i % 2)
    put("ho", 5)
    put("ro0", 6)
    put("ro1", 7)
    return where, count


def constants():
    t = np.arange(P)
    masks = []
    for h in HALVES:
        same = (t[:, None] // (2 * h)) == (t[None, :] // (2 * h))
        masks.append(same & ((t[:, None] // h) != (t[None, :] // h)))
    masks.append(np.eye(P, dtype=bool))
    n_f = DK // 4
    freqs = np.float32(10000.0) ** (-np.arange(n_f, dtype=np.float32) / np.float32(n_f))
    pos = np.arange(L)
    row, col = (pos // GRID_W).astype(np.float32), (pos % GRID_W).astype(np.float32)
    ang = np.concatenate([row[:, None] * freqs, col[:, None] * freqs], axis=-1).astype(np.float32)
    cos, sin = np.cos(ang).T.astype(np.float32), np.sin(ang).T.astype(np.float32)
    u = np.arange(7 * P)[None, :] - 3 * P - t[:, None]
    s = np.arange(LC).reshape(NC, P).T
    return {
        "k_ident": np.eye(P, dtype=np.float32),
        "k_masks": np.stack(masks, axis=1).reshape(P, 8 * P).astype(np.float32),
        "k_first": np.tile((pos % P != 0).astype(np.float32), (P, 1)),
        "k_cos": np.concatenate([cos, cos], axis=0),
        "k_sin": np.concatenate([sin, -sin], axis=0),
        "k_upos": np.maximum(u, 0).astype(np.float16),
        "k_uneg": np.maximum(-u, 0).astype(np.float16),
        "k_tpos": np.tile((pos + 1).astype(np.float16), (P, 1)),
        "k_spos": np.concatenate([LC - 1 - s, s], axis=1).astype(np.float32),
    }


def build(nc, a, out):
    where, per = bank_uses()
    with ExitStack() as top:
        def sem(name):
            return top.enter_context(nc.semaphore(name))

        begun = []

        def sem_from_1(name):
            begun.append(sem(name))
            return begun[-1]

        def after(eng, s, n):
            eng.wait_ge(s, n + 1)

        def sb(stack, name, shape, dt=F32):
            return stack.enter_context(nc.sbuf_tensor(name, shape, dt))

        psum = [top.enter_context(nc.psum_tensor(f"bank{i}", [P, 512], F32)) for i in range(8)]

        def bank(i):
            return psum[i][:, :]

        def at(name):
            return bank(where[name][0])[:, 0:LC if name.endswith(".ctx") else L]

        ident = sb(top, "ident", [P, P])
        ones = sb(top, "ones", [P, 256])
        chan = sb(top, "chan", [P, P])
        heads = sb(top, "heads", [P, H, HPN])
        modt = sb(top, "modt", [P, 48, 2])
        eps = sb(top, "eps", [P, 2])
        silu_c = sb(top, "silu_c", [P, 16])
        silu_k = silu_c[:, :].rearrange("p (c k) -> p k c", k=KT)
        hx = [sb(top, n, [P, KT, L], F32R) for n in ("hx_hi", "hx_lo")]
        raw = [sb(top, f"raw{i}", [P, D]) for i in range(2)]
        whi = [sb(top, f"whi{i}", [P, D], F32R) for i in range(2)]
        wlo = [sb(top, f"wlo{i}", [P, D], F32R) for i in range(2)]
        acc = [sb(top, n, [P, KT, L]) for n in ("acc_a", "acc_b")]

        w_landed = [sem("w_landed0"), sem("w_landed1")]
        hi_done = sem("hi_done")
        lo_done = sem("lo_done")

        w_in = a["w_in"].rearrange("a (k p) n -> p (a k) n", p=P)
        x_dram = a["x"].rearrange("a (t p) d -> p (a t) d", p=P)
        ctx_dram = a["ctx"].rearrange("a (t p) d -> p (a t) d", p=P)
        wmod = a["w_mod"].rearrange("a (k p) n -> p (a k) n", p=P)

        def kp(tile, n=P):
            return tile[:, :].rearrange("p (k n) -> p k n", n=n)

        def load_slab(sp, slot, src, n, s):
            if s is not None:
                sp.wait_ge(lo_done, s + 1)
            sp.dma_start(kp(raw[slot], n), src).then_inc(w_landed[slot], 16)

        def split_hi(act, half, slot):
            act.wait_ge(w_landed[slot], half * 16 + 16)
            act.activation(whi[slot][:, :], raw[slot][:, :], ACT.Copy).then_inc(hi_done, 1)

        def split_lo(pool, s, slot):
            pool.wait_ge(hi_done, s + 1)
            pool.tensor_tensor(wlo[slot][:, :], raw[slot][:, :], whi[slot][:, :].bitcast(F32),
                               ALU.subtract).then_inc(lo_done, 1)

        def passes(pe, dst, slot, col, pair, pick, start, stop):
            cols = slice(col, col + P)
            pe.matmul(dst, whi[slot][:, cols], pick(pair[0]), start=start, stop=False)
            pe.matmul(dst, whi[slot][:, cols], pick(pair[1]), start=False, stop=False)
            return pe.matmul(dst, wlo[slot][:, cols], pick(pair[0]), start=False, stop=stop)

        full = [sem(f"full{i}") for i in range(8)]
        free = [sem_from_1(f"free{i}") for i in range(8)]
        mraw_in, mraw_used = sem("mraw_in"), sem_from_1("mraw_used")
        hp_ready = sem("hp_ready")
        ln_ready = sem("ln_ready")
        args_ready, exp_done, mul_done = sem("args_ready"), sem("exp_done"), sem("mul_done")
        rk_ready, rq_ready = sem("rk_ready"), sem("rq_ready")
        strip_arg, strip_exp = sem("strip_arg"), sem("strip_exp")
        rav_done = sem("rav_done")
        hsq_ready, hrs_ready, hy_done = sem("hsq_ready"), sem("hrs_ready"), sem_from_1("hy_done")
        rsq_ready, rrs_ready, ry_done = sem("rsq_ready"), sem("rrs_ready"), sem("ry_done")
        tail_full = [sem(f"tail_full{i}") for i in range(8)]
        tail_free = [sem_from_1(f"tail_free{i}") for i in range(8)]
        xt2_in, mod_ready, mrg_done = sem("xt2_in"), sem("mod_ready"), sem_from_1("mrg_done")
        sq_ready, sqsum_done, tail_rstd = sem("sq_ready"), sem_from_1("sqsum_done"), sem("tail_rstd")
        nt_ready, nu_ready, hx2_ready = sem("nt_ready"), sem("nu_ready"), sem("hx2_ready")
        g_done, down_used, fin_ready = sem_from_1("g_done"), sem("down_used"), sem("fin_ready")
        y_copied, y_stored = [sem("y_copied_act"), sem("y_copied_dve")], [sem("y_stored0"), sem("y_stored1")]

        with ExitStack() as main:
            hc = [sb(main, n, [P, KT, LC], F32R) for n in ("hc_hi", "hc_lo")]
            masks = sb(main, "masks", [P, 8 * P], U8)
            first = sb(main, "first", [P, L])
            cosT = sb(main, "cosT", [P, L])
            sinT = sb(main, "sinT", [P, L])
            upos = sb(main, "upos", [P, 7 * P], F16)
            uneg = sb(main, "uneg", [P, 7 * P], F16)
            tpos = sb(main, "tpos", [P, L], F16)

            with ExitStack() as st:
                xt = sb(st, "xt", [P, NT + NC, D])
                wm = [sb(st, f"wm{i}", [P, KT, 512]) for i in range(2)]
                rows = sb(st, "rows", [P, P])
                theta = sb(st, "theta", [P, 16])
                tmp = [sb(st, f"ttmp{i}", [P, 16]) for i in range(4)]
                spos = sb(st, "spos", [P, 4])
                ss = sb(st, "ss", [P, 8])
                rstd = sb(st, "rstd", [P, 8])
                junk = sb(st, "junk", [P, D])
                masks_f = sb(st, "masks_f", [P, 8 * P])
                sc1 = sb(st, "sc1", [P, KT, 2])
                u = [sb(st, f"u{i}", [P, L + LC]) for i in range(2)]
                rows_in, const_in, x_in = sem("rows_in"), sem("const_in"), sem("x_in")
                wm_in = [sem("wm_in0"), sem("wm_in1")]
                wm_used, rows_t, chan_ready, silu_ready = sem("wm_used"), sem("rows_t"), sem("chan_ready"), sem("silu_ready")
                mod_ps, mod_done, sc_ready = sem("mod_ps"), sem("mod_done"), sem("sc_ready")
                ss_ready, rstd_ready, xn_ready = sem("ss_ready"), sem("rstd_ready"), sem("xn_ready")
                tx_full, tx_free, u_ready, u_split = sem("tx_full"), sem("tx_free"), sem("u_ready"), sem("u_split")
                th_ready, th_exp, th_ln, eps_ready, hx_hi_done, lg_ready = (sem("th_ready"), sem("th_exp"), sem("th_ln"), sem("eps_ready"),
                                                                  sem("hx_hi_done"), sem("lg_ready"))
                lbs, slots_ready = sem("lbs"), sem("slots_ready")
                wctx_done = sem("wctx_done")

                with nc.Block() as block:
                    @block.sync
                    def _(sp):
                        def row(lo, n, src):
                            sp.dma_start(rows[lo:lo + n, :], src).then_inc(rows_in, 16)
                        row(PC, 8, a["c"].rearrange("a (k p) -> (a k) p", p=P))
                        row(PCC, 8, a["c_ctx"].rearrange("(k p) -> k p", p=P))
                        row(PN1, 8, a["norm1_w"].rearrange("a (k p) -> (a k) p", p=P))
                        row(PN2, 8, a["norm2_w"].rearrange("a (k p) -> (a k) p", p=P))
                        row(PFN, 8, a["final_norm_w"].rearrange("(k p) -> k p", p=P))
                        row(PHG, 8, a["hg_norm_w"].rearrange("a (k p) -> (a k) p", p=P))
                        row(PLF, 16, a["hg_lb_fwd"].rearrange("a (k p) -> (a k) p", p=P))
                        row(PLB, 16, a["hg_lb_bwd"].rearrange("a (k p) -> (a k) p", p=P))
                        row(PBM, 48, a["b_mod"].rearrange("a (k p) -> (a k) p", p=P))
                        for dst, src in ((ident, "k_ident"), (spos, "k_spos")):
                            sp.dma_start(dst[:, :], a[src]).then_inc(const_in, 16)
                        sp.dma_start(theta[:, 0:8], a["rt_theta_fwd"].to_broadcast([P, 8])).then_inc(const_in, 16)
                        sp.dma_start(theta[:, 8:16], a["rt_theta_bwd"].to_broadcast([P, 8])).then_inc(const_in, 16)
                        sp.dma_start(wm[0][:, :, :], wmod[:, :, 0:512]).then_inc(wm_in[0], 16)
                        sp.dma_start(xt[:, 0:NT, :], x_dram).then_inc(x_in, 16)
                        sp.dma_start(xt[:, NT:NT + NC, :], ctx_dram).then_inc(x_in, 16)
                        sp.dma_start(wm[1][:, :, :], wmod[:, :, 512:1024]).then_inc(wm_in[1], 16)
                        for j in (2, 3):
                            sp.wait_ge(wm_used, j - 1)
                            sp.dma_start(wm[j % 2][:, :, :], wmod[:, :, j * 512:(j + 1) * 512]).then_inc(wm_in[j % 2], 16)
                        for dst, src in ((masks_f, "k_masks"), (first, "k_first"), (cosT, "k_cos"), (sinT, "k_sin"),
                                         (upos, "k_upos"), (uneg, "k_uneg"), (tpos, "k_tpos")):
                            sp.dma_start(dst[:, :], a[src]).then_inc(const_in, 16)
                        for slot in range(2):
                            _, col, step, tile, _ = SLABS[slot]
                            sp.dma_start(kp(raw[slot]), w_in[:, :, col + tile * P:col + (tile + 1) * P]).then_inc(w_landed[slot], 16)
                        sp.wait_ge(const_in, 16 * 11)

                    @block.gpsimd
                    def _(pool):
                        pool.memset(acc[0][:, :, :], 0.0).then_inc(slots_ready, 1)
                        pool.memset(acc[1][:, :, :], 0.0).then_inc(lo_done, 1)
                        pool.memset(ones[:, :], 1.0).then_inc(lo_done, 1)
                        for s in begun:
                            pool.nop().then_inc(s, 1)
                        for slot in range(2):
                            split_lo(pool, slot, slot)

                    @block.tensor
                    def _(pe):
                        pe.wait_ge(rows_in, 16 * 9)
                        pe.wait_ge(const_in, 16 * 4)
                        pe.transpose(psum[0][:, 0:P], rows[:, :], ident[:, :]).then_inc(rows_t, 1)
                        pe.wait_ge(silu_ready, 1)
                        for j in range(4):
                            pe.wait_ge(wm_in[j % 2], 16 * (j // 2 + 1))
                            for t in range(4):
                                for k in range(KT):
                                    m = pe.matmul(psum[1][:, (4 * j + t) * 2:(4 * j + t) * 2 + 2], wm[j % 2][:, k, t * P:(t + 1) * P],
                                                  silu_k[:, k, :], start=(k == 0), stop=(k == KT - 1))
                            m.then_inc(wm_used, 1)
                            if j == 0:
                                pe.wait_ge(xn_ready, NT + NC)
                        for k in range(KT):
                            b = 2 + 2 * (k % 2)
                            if k >= 2:
                                pe.wait_ge(tx_free, k - 1)
                            for t in range(NT + NC):
                                m = pe.transpose(psum[b + t // 4][:, (t % 4) * P:(t % 4 + 1) * P], xt[:, t, k * P:(k + 1) * P], ident[:, :])
                            m.then_inc(tx_full, 1)

                    @block.scalar
                    def _(act):
                        act.wait_ge(chan_ready, 1)
                        act.activation(silu_c[:, :], chan[:, PC:PC + 16], ACT.Silu).then_inc(silu_ready, 1)
                        act.wait_ge(x_in, 32)
                        for t in range(NT + NC):
                            act.activation(junk[:, :], xt[:, t, :], ACT.Square, accum_out=ss[:, t:t + 1]).then_inc(ss_ready, 1)
                            act.drain()
                        act.wait_ge(eps_ready, 2)
                        act.activation(rstd[:, 0:6], ss[:, 0:6], ACT.Ln, bias=eps[:, 0:1], scale=1.0 / D)
                        act.drain()
                        act.activation(rstd[:, 0:6], rstd[:, 0:6], ACT.Exp, scale=-0.5).then_inc(rstd_ready, 1)
                        act.wait_ge(th_ready, 1)
                        act.activation(tmp[0][:, :], tmp[0][:, :], ACT.Exp, scale=-1.0).then_inc(th_exp, 1)
                        act.wait_ge(th_ready, 2)
                        act.activation(tmp[2][:, :], tmp[1][:, :], ACT.Ln).then_inc(th_ln, 1)
                        act.wait_ge(lg_ready, 1)
                        for h in range(H):
                            act.activation(heads[:, h, WC:WC + 2], spos[:, 0:2], ACT.Exp, scale=heads[:, h, LGF:LGF + 1])
                            act.activation(heads[:, h, WC + 2:WC + 4], spos[:, 2:4], ACT.Exp, scale=heads[:, h, LGB:LGB + 1]).then_inc(wctx_done, 1)
                        act.wait_ge(lbs, 1)
                        for dst, src, sc in ((LBF, 0, 1.0), (OMF, 0, -1.0), (LBB, 1, 1.0), (OMB, 1, -1.0)):
                            act.activation(heads[:, :, dst], tmp[3][:, 8 * src:8 * src + 8], ACT.Sigmoid, scale=sc)
                        for slot in range(2):
                            split_hi(act, 0, slot)
                        act.wait_ge(sc_ready, 1)
                        for k in range(KT):
                            act.wait_ge(tx_full, k + 1)
                            if k >= 2:
                                act.wait_ge(u_split, k - 1)
                            b = 2 + 2 * (k % 2)
                            act.activation(u[k % 2][:, 0:L], psum[b][:, :], ACT.Identity, bias=modt[:, k, 0:1], scale=sc1[:, k, 0:1])
                            act.activation(u[k % 2][:, L:L + LC], psum[b + 1][:, 0:LC], ACT.Identity, bias=modt[:, k, 1:2],
                                           scale=sc1[:, k, 1:2]).then_inc(tx_free, 1)

                    @block.vector
                    def _(dve):
                        dve.memset(eps[:, 0:1], EPS).then_inc(eps_ready, 1)
                        dve.memset(eps[:, 1:2], GN_EPS).then_inc(eps_ready, 1)
                        dve.wait_ge(rows_t, 1)
                        dve.tensor_copy(chan[:, :], psum[0][:, 0:P]).then_inc(chan_ready, 1)
                        dve.wait_ge(const_in, 16 * 4)
                        dve.tensor_scalar(tmp[0][:, :], theta[:, :], -80.0, None, ALU.max).then_inc(th_ready, 1)
                        dve.wait_ge(th_exp, 1)
                        dve.tensor_scalar(tmp[1][:, :], tmp[0][:, :], 1.0, None, ALU.add).then_inc(th_ready, 1)
                        dve.wait_ge(th_ln, 1)
                        dve.drain()
                        dve.tensor_scalar(tmp[3][:, :], tmp[1][:, :], -1.0, None, ALU.add)
                        dve.drain()
                        dve.tensor_scalar(tmp[1][:, :], tmp[3][:, :], 0.0, None, ALU.is_equal)
                        dve.drain()
                        dve.tensor_tensor(tmp[3][:, :], tmp[3][:, :], tmp[1][:, :], ALU.add)
                        dve.tensor_tensor(tmp[2][:, :], tmp[2][:, :], tmp[1][:, :], ALU.add)
                        dve.drain()
                        dve.reciprocal(tmp[3][:, :], tmp[3][:, :])
                        dve.tensor_tensor(tmp[2][:, :], tmp[2][:, :], tmp[0][:, :], ALU.mult)
                        dve.drain()
                        dve.tensor_tensor(tmp[2][:, :], tmp[2][:, :], tmp[3][:, :], ALU.mult)
                        dve.drain()
                        for d, dst in ((0, LGF), (1, LGB)):
                            m = dve.tensor_scalar(heads[:, :, dst], tmp[2][:, 8 * d:8 * d + 8], -1.0, None, ALU.mult)
                        m.then_inc(lg_ready, 1)
                        dve.tensor_copy(heads[:, :, HGN], chan[:, PHG:PHG + 8])
                        dve.tensor_tensor(tmp[3][:, 0:8], chan[:, PLF:PLF + 8], chan[:, PLF + 8:PLF + 16], ALU.subtract)
                        dve.tensor_tensor(tmp[3][:, 8:16], chan[:, PLB:PLB + 8], chan[:, PLB + 8:PLB + 16], ALU.subtract).then_inc(lbs, 1)
                        dve.wait_ge(rstd_ready, 1)
                        for t in range(NT + NC):
                            dve.tensor_scalar(xt[:, t, :], xt[:, t, :], rstd[:, t:t + 1], None, ALU.mult).then_inc(xn_ready, 1)
                        dve.wait_ge(wm_used, 4)
                        dve.tensor_tensor(modt[:, 0:16, :], psum[1][:, 0:32].rearrange("p (t c) -> p t c", c=2),
                                          chan[:, PBM:PBM + 16].unsqueeze(2).to_broadcast([P, 16, 2]), ALU.add)
                        dve.drain()
                        dve.scalar_tensor_tensor(out=sc1[:, :, :], in0=modt[:, 8:16, :], scalar=1.0,
                                                 in1=chan[:, PN1:PN1 + 8].unsqueeze(2).to_broadcast([P, 8, 2]),
                                                 op0=ALU.add, op1=ALU.mult).then_inc(sc_ready, 1)
                        dve.wait_ge(const_in, 16 * 11)
                        dve.tensor_copy(masks[:, :], masks_f[:, :])
                        for k in range(KT):
                            dve.wait_ge(tx_free, k + 1)
                            dve.tensor_copy(hx[0][:, k, :], u[k % 2][:, 0:L])
                            dve.tensor_copy(hc[0][:, k, :], u[k % 2][:, L:L + LC])
                            dve.drain()
                            dve.tensor_tensor(hx[1][:, k, :], u[k % 2][:, 0:L], hx[0][:, k, :].bitcast(F32), ALU.subtract)
                            dve.tensor_tensor(hc[1][:, k, :], u[k % 2][:, L:L + LC], hc[0][:, k, :].bitcast(F32), ALU.subtract).then_inc(u_split, 1)

            with ExitStack() as st:
                mraw = sb(st, "mraw", [P, KT, P])
                hp = sb(st, "hp", [P, HPN])
                q, kf, kb, bf, bb = [sb(st, n, [P, L]) for n in ("q", "kf", "kb", "bf", "bb")]
                kfc, kbc, gfc, gbc = [sb(st, n, [P, LC]) for n in ("kfc", "kbc", "gfc", "gbc")]
                vT = sb(st, "vT", [P, L + LC])
                v = sb(st, "v", [P, NT + NC, P])
                E = [sb(st, f"E{i}", [P, 2 * L]) for i in range(2)]
                att = sb(st, "att", [P, L])
                kTc = sb(st, "kTc", [P, 4, P])
                kTf, kTb = sb(st, "kTf", [P, 3, P]), sb(st, "kTb", [P, 3, P])
                Sf, Sb = sb(st, "Sf", [P, NT, P]), sb(st, "Sb", [P, NT, P])
                cdec = sb(st, "cdec", [P, 2, NT])
                rq, rk = sb(st, "rq", [P, L]), sb(st, "rk", [P, L])
                rkc = sb(st, "rkc", [P, LC])
                rv = sb(st, "rv", [P, NT + NC, 2 * P])
                ratt = [sb(st, f"ratt{i}", [P, L]) for i in range(2)]
                strip = sb(st, "strip", [P, 7 * P])
                kw = sb(st, "kw", [P, 4, P])
                rS = sb(st, "rS", [P, 4, P])
                gate = [sb(st, f"gate{i}", [P, L]) for i in range(3)]
                y = [sb(st, n, [P, 3, L], F32R) for n in ("y_hi", "y_lo")]

                EXPS = {0: 0, 1: 1, 2: 2, 3: 3, 4: 4, 5: 5, 6: 6, 7: 7, 9: 8, 10: 9, 11: 10}
                ARGS = {0: 0, 1: 1, 2: 2, 3: 3, 4: 4, 5: 5, 6: 6, 7: 7, 9: 8, 10: 9}
                NJ = 12

                def wait_full(eng, name, h):
                    b, n = where[name]
                    eng.wait_ge(full[b], h * per[b] + n + 1)

                def wait_free(pe, name, h, *copied):
                    need = dict([where[name]])
                    for other in copied:
                        b, n = where[other]
                        need[b] = max(need.get(b, 0), n + 1)
                    for b, n in need.items():
                        after(pe, free[b], h * per[b] + n)

                def wait_emptied(eng, name, h):
                    b, n = where[name]
                    after(eng, free[b], h * per[b] + n + 1)

                def halves(t, h):
                    return t.rearrange("p (b s h) -> p b s h", s=2, h=h)

                def chunks(t):
                    return t.rearrange("p (c t) -> p c t", t=P)

                with nc.Block() as block:
                    @block.sync
                    def _(sp):
                        def mod_load(h, m):
                            tile = h * 4 + (16 + m)
                            after(sp, mraw_used, h * 4 + m)
                            sp.dma_start(mraw[:, :, :], wmod[:, :, bass.ds(tile * P, P)]).then_inc(mraw_in, 16)

                        with sp.Fori(0, H) as h:
                            for j in range(NSLAB):
                                i = j + 2
                                s = h * NSLAB + i
                                slot = i % 2
                                if j < 4:
                                    mod_load(h, j)
                                if i == GEMM["b"]:
                                    s = s + 1
                                elif i == GEMM["q"]:
                                    s = None
                                if i >= NSLAB or i < len(SLABS):
                                    _, col, step, tile, _ = SLABS[i % NSLAB]
                                    if i >= NSLAB:
                                        col += step
                                    load_slab(sp, slot, w_in[:, :, bass.ds(h * step + (col + tile * P), P)], P, s)
                                elif i == len(SLABS):
                                    load_slab(sp, slot, a["w_proj_hgrn"].rearrange("a (k p) n -> p (a k) n", p=P)[:, bass.ds(h, 1), :], D, s)
                                else:
                                    half = i - len(SLABS) - 1
                                    src = a["w_proj_ret"].rearrange("a (k p) n -> p (a k) n", p=P)
                                    load_slab(sp, slot, src[:, bass.ds(h * 2, 2), half * 512:(half + 1) * 512], 512, s)

                    @block.gpsimd
                    def _(pool):
                        with pool.Fori(0, H) as h:
                            for j in range(2, NSLAB + 2):
                                split_lo(pool, h * NSLAB + j, j % 2)

                    @block.tensor
                    def _(pe):
                        def gemm(h, name, part):
                            j = GEMM[name]
                            slot = j % 2
                            if part == "a":
                                pe.wait_ge(lo_done, h * NSLAB + (j + 3))
                                wait_free(pe, name, h)
                            if part == "c":
                                wait_free(pe, name + ".ctx", h)
                                for k in range(KT):
                                    m = passes(pe, at(name + ".ctx"), slot, k * P, hc, lambda t: t[:, k, :], k == 0, k == KT - 1)
                                m.then_inc(full[where[name + ".ctx"][0]], 1)
                                return
                            for k in (range(KT // 2) if part == "a" else range(KT // 2, KT)):
                                m = passes(pe, at(name), slot, k * P, hx, lambda t: t[:, k, :], k == 0, k == KT - 1)
                            if part == "b":
                                m.then_inc(full[where[name][0]], 1)

                        def transposes(h, name, src, n, *copied):
                            wait_free(pe, name, h, *copied)
                            for t in range(n):
                                m = pe.transpose(at(name)[:, t * P:(t + 1) * P], src(t), ident[:, :])
                            m.then_inc(full[where[name][0]], 1)

                        def project(h, j, name, tiles, ys):
                            slot = j % 2
                            pe.wait_ge(lo_done, h * NSLAB + (j + 3))
                            for i, n in enumerate(tiles):
                                wait_free(pe, f"{name}{n}", h)
                                for k, yt in enumerate(ys):
                                    c = k * 512 + i * P
                                    m = passes(pe, at(f"{name}{n}"), slot, c, y, lambda t: t[:, yt, :], k == 0, k == len(ys) - 1)
                                m.then_inc(full[where[f"{name}{n}"][0]], 1)

                        with pe.Fori(0, H) as h:
                            for step in STEPS:
                                name, _, part = step.partition(".")
                                if name in GEMM and part in ("a", "b", "c"):
                                    gemm(h, name, part)
                                elif name.startswith("mod"):
                                    m_ = int(name[3:])
                                    pe.wait_ge(mraw_in, h * 64 + (16 * m_ + 16))
                                    wait_free(pe, name + ".ctx", h)
                                    for k in range(KT):
                                        m = pe.matmul(at(name + ".ctx")[:, 0:2], mraw[:, k, :], silu_k[:, k, :], start=(k == 0), stop=(k == KT - 1))
                                    m.then_inc(full[where[name + ".ctx"][0]], 1)
                                elif name in ("Tv", "Trv0", "Trv1"):
                                    transposes(h, name, lambda t: vT[:, t * P:(t + 1) * P], NT, name[1:], name[1:] + ".ctx")
                                    transposes(h, name + "c", lambda t: vT[:, L + t * P:L + (t + 1) * P], NC)
                                elif name == "job0":
                                    pe.wait_ge(mul_done, h * NJ + 1)
                                    transposes(h, "job0", lambda t: E[0][:, t * P:(t + 1) * P], 4)
                                elif name == "KVc":
                                    wait_free(pe, name, h, "job0", "Tv", "Tvc")
                                    for d in range(2):
                                        for c in range(NC):
                                            m = pe.matmul(at(name)[:, d * P:(d + 1) * P], kTc[:, NC * d + c, :], v[:, NT + c, :],
                                                          start=(c == 0), stop=(c == NC - 1))
                                    m.then_inc(full[where[name][0]], 1)
                                elif name in ("job9", "job10"):
                                    j = int(name[3:])
                                    pe.wait_ge(mul_done, h * NJ + (j + 1))
                                    order = [0, 1, 2] if j == 9 else [3, 2, 1]
                                    transposes(h, name, lambda t: E[j % 2][:, L + order[t] * P:L + (order[t] + 1) * P], 3)
                                elif name.startswith("job"):
                                    j = int(name[3:])
                                    pe.wait_ge(mul_done, h * NJ + (j + 1))
                                    wait_free(pe, name, h)
                                    for c in range(NT):
                                        rhs = q[:, c * P:(c + 1) * P] if j == 8 else E[j % 2][:, c * P:(c + 1) * P]
                                        m = pe.matmul(at(name)[:, c * P:(c + 1) * P], E[j % 2][:, L + c * P:L + (c + 1) * P], rhs, start=True, stop=True)
                                    m.then_inc(full[where[name][0]], 1)
                                elif name in ("KVf", "KVb"):
                                    f = name == "KVf"
                                    wait_free(pe, name, h, "job9" if f else "job10")
                                    for i, c in enumerate([0, 1, 2] if f else [3, 2, 1]):
                                        m = pe.matmul(at(name)[:, i * P:(i + 1) * P], (kTf if f else kTb)[:, i, :], v[:, c, :], start=True, stop=True)
                                    m.then_inc(full[where[name][0]], 1)
                                elif name == "rkT":
                                    transposes(h, name, lambda t: rkc[:, t * P:(t + 1) * P], NC, "rk.ctx")
                                elif name == "rKV":
                                    wait_free(pe, name, h, "rkT", "Trv1", "Trv1c")
                                    for d in range(2):
                                        for c in range(NC):
                                            m = pe.matmul(at(name)[:, d * 256:(d + 1) * 256], kw[:, NC * d + c, :], rv[:, NT + c, :],
                                                          start=(c == 0), stop=(c == NC - 1))
                                    m.then_inc(full[where[name][0]], 1)
                                elif name.startswith("att"):
                                    i = int(name[3:])
                                    if i == 0:
                                        pe.wait_ge(rk_ready, h + 1)
                                        pe.wait_ge(rq_ready, h + 1)
                                    wait_free(pe, name, h)
                                    pe.matmul(at(name), rk[:, i * P:(i + 1) * P], rq[:, :], start=True, stop=True).then_inc(full[where[name][0]], 1)
                                elif name.startswith("av"):
                                    i = int(name[2:])
                                    if i == 0:
                                        wait_free(pe, "ro0", h)
                                        wait_free(pe, "ro1", h)
                                    wait_emptied(pe, f"att{i}", h)
                                    for e in range(2):
                                        m = pe.matmul(at(f"ro{e}"), rv[:, i, e * P:(e + 1) * P], ratt[i % 2][:, :], start=(i == 0), stop=False)
                                    m.then_inc(rav_done, 1)
                                elif name == "rstate":
                                    wait_emptied(pe, "rKV", h)
                                    pe.wait_ge(mul_done, h * NJ + 12)
                                    for e in range(2):
                                        for d in range(2):
                                            m = pe.matmul(at(f"ro{e}"), rS[:, 2 * d + e, :], E[1][:, d * L:(d + 1) * L], start=False, stop=(d == 1))
                                        m.then_inc(full[6 + e], 1)
                                elif name == "hgo":
                                    wait_free(pe, "ho", h, "job8", "KVf", "KVb")
                                    for c in range(NT):
                                        cs = slice(c * P, (c + 1) * P)
                                        pe.matmul(at("ho")[:, cs], v[:, c, :], att[:, cs], start=True, stop=False)
                                        pe.matmul(at("ho")[:, cs], Sf[:, c, :], bf[:, cs], start=False, stop=False)
                                        m = pe.matmul(at("ho")[:, cs], Sb[:, c, :], bb[:, cs], start=False, stop=True)
                                    m.then_inc(full[5], 1)
                                elif name == "hstat":
                                    pe.wait_ge(hsq_ready, h + 1)
                                    wait_free(pe, name, h)
                                    pe.matmul(at(name), ones[:, 0:P], kf[:, :], start=True, stop=True).then_inc(full[where[name][0]], 1)
                                elif name == "rmean":
                                    wait_free(pe, name, h, "ro0", "ro1")
                                    pe.matmul(at(name), ones[:, 0:P], ratt[0][:, :], start=True, stop=False)
                                    pe.matmul(at(name), ones[:, 0:P], ratt[1][:, :], start=False, stop=True).then_inc(full[where[name][0]], 1)
                                elif name == "rvar":
                                    pe.wait_ge(rsq_ready, h + 1)
                                    wait_free(pe, name, h)
                                    pe.matmul(at(name), ones[:, 0:P], rk[:, :], start=True, stop=False)
                                    pe.matmul(at(name), ones[:, 0:P], rq[:, :], start=False, stop=True).then_inc(full[where[name][0]], 1)
                                elif name == "pa":
                                    after(pe, hy_done, h + 1)
                                    project(h, len(SLABS), "pa", range(8), [0])
                                elif name == "pb":
                                    pe.wait_ge(ry_done, h + 1)
                                    for half in range(2):
                                        project(h, len(SLABS) + 1 + half, "pb", range(4 * half, 4 * half + 4), [1, 2])

                    @block.scalar
                    def _(act):
                        with act.Fori(0, H) as h:
                            for step in STEPS:
                                name, _, part = step.partition(".")
                                if step in ("rg0.d", "rg1.d", "g.d"):
                                    i = ("rg0", "rg1", "g").index(name)
                                    wait_full(act, name, h)
                                    act.activation(gate[i][:, :], at(name), ACT.Silu).then_inc(free[where[name][0]], 1)
                                elif step in ("f.d", "b.d"):
                                    wait_full(act, name, h)
                                    after(act, hy_done, h)
                                    act.activation((bf if name == "f" else bb)[:, :], at(name), ACT.Sigmoid)
                                    act.activation((kf if name == "f" else kb)[:, :], at(name), ACT.Sigmoid, scale=-1.0).then_inc(free[where[name][0]], 1)
                                elif step in ("f.e", "b.e"):
                                    src = name + ".ctx"
                                    wait_full(act, src, h)
                                    act.activation((gfc if name == "f" else gbc)[:, :], at(src), ACT.Sigmoid)
                                    act.activation((kfc if name == "f" else kbc)[:, :], at(src), ACT.Sigmoid, scale=-1.0).then_inc(free[where[src][0]], 1)
                                elif step == "gates":
                                    act.drain()
                                    act.wait_ge(hp_ready, h + 1)
                                    for t, lb, om in ((gfc, LBF, OMF), (gbc, LBB, OMB), (bf, LBF, OMF), (bb, LBB, OMB)):
                                        m = act.activation(t[:, :], t[:, :], ACT.Ln, bias=hp[:, lb:lb + 1], scale=hp[:, om:om + 1])
                                    m.then_inc(ln_ready, 1)
                                elif step == "strip":
                                    act.wait_ge(strip_arg, h + 1)
                                    act.activation(strip[:, :], strip[:, :], ACT.Exp).then_inc(strip_exp, 1)
                                elif step == "q.d":
                                    wait_full(act, name, h)
                                    act.activation(q[:, :], at(name), ACT.Copy, scale=QSCALE).then_inc(free[where[name][0]], 1)
                                elif step in ("v.d", "rv0.d", "rv1.d"):
                                    wait_full(act, name, h)
                                    act.activation(vT[:, 0:L], at(name), ACT.Copy).then_inc(free[where[name][0]], 1)
                                elif step in ("v.e", "rv0.e", "rv1.e"):
                                    wait_full(act, name + ".ctx", h)
                                    act.activation(vT[:, L:L + LC], at(name + ".ctx"), ACT.Copy).then_inc(free[where[name + ".ctx"][0]], 1)
                                elif step == "rk.e":
                                    wait_full(act, "rk.ctx", h)
                                    act.activation(rkc[:, :], at("rk.ctx"), ACT.Copy).then_inc(free[where["rk.ctx"][0]], 1)
                                elif step == "Tv":
                                    wait_full(act, "Tv", h)
                                    act.activation(v[:, 0:NT, :], chunks(at("Tv")), ACT.Copy).then_inc(free[where["Tv"][0]], 1)
                                    wait_full(act, "Tvc", h)
                                    act.activation(v[:, NT:NT + NC, :], chunks(at("Tvc")[:, 0:LC]), ACT.Copy).then_inc(free[where["Tvc"][0]], 1)
                                elif step in ("Trv0", "Trv1"):
                                    e = int(step[-1])
                                    wait_full(act, step, h)
                                    act.activation(rv[:, 0:NT, e * P:(e + 1) * P], chunks(at(step)), ACT.Copy).then_inc(free[where[step][0]], 1)
                                    wait_full(act, step + "c", h)
                                    act.activation(rv[:, NT:NT + NC, e * P:(e + 1) * P], chunks(at(step + "c")[:, 0:LC]), ACT.Copy)\
                                        .then_inc(free[where[step + "c"][0]], 1)
                                elif name.startswith("prep"):
                                    j = int(name[4:])
                                    e = E[j % 2]
                                    if j in ARGS:
                                        act.wait_ge(args_ready, h * len(ARGS) + (ARGS[j] + 1))
                                    if j == 0:
                                        act.activation(e[:, 0:L], e[:, 0:L], ACT.Exp).then_inc(exp_done, 1)
                                    elif 1 <= j <= 7:
                                        act.activation(e[:, :], e[:, :], ACT.Exp).then_inc(exp_done, 1)
                                    elif j in (9, 10):
                                        act.activation(e[:, 0:L], (bf if j == 9 else bb)[:, :], ACT.Exp)
                                        act.activation(e[:, L:2 * L], e[:, L:2 * L], ACT.Exp).then_inc(exp_done, 1)
                                    elif j == 11:
                                        wait_full(act, "job9", h)
                                        act.activation(e[:, 0:L], tpos[:, :], ACT.Exp, scale=hp[:, LGF:LGF + 1])
                                        act.activation(e[:, L:2 * L], tpos[:, ::-1], ACT.Exp, scale=hp[:, LGB:LGB + 1]).then_inc(exp_done, 1)
                                elif step in ("job0", "job9", "job10"):
                                    wait_full(act, step, h)
                                    dst, n = {"job0": (kTc, 4), "job9": (kTf, 3), "job10": (kTb, 3)}[step]
                                    act.activation(dst[:, :, :], chunks(at(step)[:, 0:n * P]), ACT.Copy).then_inc(free[where[step][0]], 1)
                                elif step == "rkT":
                                    wait_full(act, step, h)
                                    for d in range(2):
                                        for c in range(NC):
                                            m = act.activation(kw[:, NC * d + c, :], at(step)[:, c * P:(c + 1) * P], ACT.Copy,
                                                               scale=hp[:, WC + NC * d + c:WC + NC * d + c + 1])
                                    m.then_inc(free[where[step][0]], 1)
                                elif step == "rKV":
                                    wait_full(act, step, h)
                                    act.activation(rS[:, :, :], chunks(at(step)), ACT.Copy).then_inc(free[where[step][0]], 1)
                                elif step == "hstat":
                                    wait_full(act, "ho", h)
                                    act.activation(kf[:, :], at("ho"), ACT.Square).then_inc(hsq_ready, 1)
                                elif step == "rmean":
                                    wait_full(act, "ro0", h)
                                    act.activation(ratt[0][:, :], at("ro0"), ACT.Copy).then_inc(free[6], 1)
                                    wait_full(act, "ro1", h)
                                    act.activation(ratt[1][:, :], at("ro1"), ACT.Copy).then_inc(free[7], 1)
                                elif step == "hnorm":
                                    wait_full(act, "hstat", h)
                                    act.activation(kb[:, :], at("hstat"), ACT.Ln, bias=eps[:, 0:1], scale=1.0 / P).then_inc(free[where["hstat"][0]], 1)
                                    act.drain()
                                    act.activation(kb[:, :], kb[:, :], ACT.Exp, scale=-0.5).then_inc(hrs_ready, 1)
                                elif step == "rvar":
                                    wait_emptied(act, "rmean", h)
                                    act.activation(rk[:, :], ratt[0][:, :], ACT.Square)
                                    act.activation(rq[:, :], ratt[1][:, :], ACT.Square).then_inc(rsq_ready, 1)
                                elif step == "rnorm":
                                    wait_full(act, "rvar", h)
                                    act.activation(rq[:, :], at("rvar"), ACT.Ln, bias=eps[:, 1:2], scale=1.0 / (2 * P)).then_inc(free[where["rvar"][0]], 1)
                                    act.drain()
                                    act.activation(rq[:, :], rq[:, :], ACT.Exp, scale=-0.5).then_inc(rrs_ready, 1)
                                last = {"pa": [("pa7", 11)], "pb": [("pb3", 12), ("pb7", 13)]}.get(step, [])
                                if name in GEMM and part == ("e" if SLABS[GEMM[name]][4] else "d"):
                                    last = [(name + (".ctx" if part == "e" else ""), GEMM[name])]
                                for product, j in last:
                                    wait_full(act, product, h)
                                    split_hi(act, h * (NSLAB // 2) + (j // 2 + 1), j % 2)

                    @block.vector
                    def _(dve):
                        def rope(h, name, dst, scale, ready):
                            wait_full(dve, name, h)
                            ps = at(name)
                            tmp = ratt[0]
                            dve.scalar_tensor_tensor(out=dst[:, :], in0=ps, scalar=scale, in1=cosT[:, :], op0=ALU.mult, op1=ALU.mult)
                            dve.scalar_tensor_tensor(out=tmp[64:P, :], in0=ps[0:64, :], scalar=scale, in1=sinT[0:64, :], op0=ALU.mult, op1=ALU.mult)
                            dve.scalar_tensor_tensor(out=tmp[0:64, :], in0=ps[64:P, :], scalar=scale, in1=sinT[64:P, :], op0=ALU.mult,
                                                     op1=ALU.mult).then_inc(free[where[name][0]], 1)
                            dve.drain()
                            dve.tensor_tensor(dst[:, :], dst[:, :], tmp[:, :], ALU.add).then_inc(ready, 1)

                        def accumulate(h, name, tiles, dst):
                            for n in tiles:
                                wait_full(dve, f"{name}{n}", h)
                                dve.tensor_tensor(dst[:, n, :], dst[:, n, :], at(f"{name}{n}"), ALU.add).then_inc(free[where[f"{name}{n}"][0]], 1)

                        with dve.Fori(0, H) as h:
                            dve.tensor_copy(hp[:, :], heads[:, bass.ds(h, 1), :].rearrange("p a n -> p (a n)")).then_inc(hp_ready, 1)
                            for step in STEPS:
                                name, _, part = step.partition(".")
                                if name.startswith("mod"):
                                    wait_full(dve, name + ".ctx", h)
                                    dve.nop().then_inc(mraw_used, 1)
                                    m_ = int(name[3:])
                                    dve.tensor_copy(modt[:, bass.ds(h * 4 + (16 + m_), 1), :].rearrange("p a n -> p (a n)"),
                                                    at(name + ".ctx")[:, 0:2]).then_inc(free[where[name + ".ctx"][0]], 1)
                                elif step == "gates":
                                    dve.wait_ge(ln_ready, h + 1)
                                    e = E[0]
                                    dve.memset(e[:, LC - 1:LC + 1], 0.0)
                                    dve.tensor_tensor_scan(e[:, LC - 2::-1], ones[:, 0:LC - 1], gfc[:, LC - 1:0:-1], 0.0, ALU.mult, ALU.add)
                                    dve.tensor_tensor_scan(e[:, LC + 1:2 * LC], ones[:, 0:LC - 1], gbc[:, 0:LC - 1], 0.0, ALU.mult, ALU.add)\
                                        .then_inc(args_ready, 1)
                                    for t, om in ((kfc, OMF), (kbc, OMB), (kf, OMF), (kb, OMB)):
                                        dve.tensor_scalar(t[:, :], t[:, :], hp[:, om:om + 1], None, ALU.mult)
                                    dve.tensor_tensor_scan(bf[:, :], first[:, :], bf[:, :], 0.0, ALU.mult, ALU.add)
                                    dve.tensor_tensor_scan(bb[:, ::-1], first[:, :], bb[:, ::-1], 0.0, ALU.mult, ALU.add)
                                    dve.drain()
                                elif step == "strip":
                                    dve.tensor_scalar(strip[:, :], upos[:, :], hp[:, LGF:LGF + 1], None, ALU.mult)
                                    dve.drain()
                                    dve.scalar_tensor_tensor(out=strip[:, :], in0=uneg[:, :], scalar=hp[:, LGB:LGB + 1], in1=strip[:, :],
                                                             op0=ALU.mult, op1=ALU.add).then_inc(strip_arg, 1)
                                elif name.startswith("prep"):
                                    j = int(name[4:])
                                    e = E[j % 2]
                                    if 1 <= j <= 7:
                                        if j >= 2:
                                            wait_full(dve, f"job{j - 2}", h)
                                        hh = HALVES[j - 1]
                                        nb = L // (2 * hh)
                                        eq, ek = halves(e[:, 0:L], hh), halves(e[:, L:2 * L], hh)
                                        f_, b_ = halves(bf[:, :], hh), halves(bb[:, :], hh)
                                        fm = f_[:, :, 0, hh - 1:hh].to_broadcast([P, nb, hh])
                                        bm = b_[:, :, 1, 0:1].to_broadcast([P, nb, hh])
                                        dve.tensor_tensor(eq[:, :, 1, :], f_[:, :, 1, :], fm, ALU.subtract)
                                        dve.tensor_tensor(eq[:, :, 0, :], b_[:, :, 0, :], bm, ALU.subtract)
                                        dve.tensor_tensor(ek[:, :, 0, :], fm, f_[:, :, 0, :], ALU.subtract)
                                        dve.tensor_tensor(ek[:, :, 1, :], bm, b_[:, :, 1, :], ALU.subtract).then_inc(args_ready, 1)
                                    elif j in (9, 10):
                                        wait_full(dve, f"job{j - 2}", h)
                                        src = chunks((bf if j == 9 else bb)[:, :])
                                        edge = src[:, :, P - 1:P] if j == 9 else src[:, :, 0:1]
                                        dve.tensor_tensor(chunks(e[:, L:2 * L]), edge.to_broadcast([P, NT, P]), src, ALU.subtract).then_inc(args_ready, 1)
                                elif name.startswith("mul"):
                                    j = int(name[3:])
                                    e = E[j % 2]
                                    if j in EXPS:
                                        dve.wait_ge(exp_done, h * len(EXPS) + (EXPS[j] + 1))
                                    if j == 0:
                                        dve.tensor_tensor(e[:, 0:LC], e[:, 0:LC], kfc[:, :], ALU.mult)
                                        dve.tensor_tensor(e[:, LC:2 * LC], e[:, LC:2 * LC], kbc[:, :], ALU.mult).then_inc(mul_done, 1)
                                    elif 1 <= j <= 7:
                                        hh = HALVES[j - 1]
                                        ek, f_, b_ = halves(e[:, L:2 * L], hh), halves(kf[:, :], hh), halves(kb[:, :], hh)
                                        if j == 1:
                                            wait_emptied(dve, "q", h)
                                        dve.tensor_tensor(e[:, 0:L], e[:, 0:L], q[:, :], ALU.mult)
                                        dve.tensor_tensor(ek[:, :, 0, :], ek[:, :, 0, :], f_[:, :, 0, :], ALU.mult)
                                        dve.tensor_tensor(ek[:, :, 1, :], ek[:, :, 1, :], b_[:, :, 1, :], ALU.mult).then_inc(mul_done, 1)
                                    elif j == 8:
                                        wait_full(dve, "job6", h)
                                        dve.tensor_tensor(e[:, L:2 * L], kf[:, :], kb[:, :], ALU.add).then_inc(mul_done, 1)
                                    elif j in (9, 10):
                                        k_, s_ = (kf, bf) if j == 9 else (kb, bb)
                                        d = j - 9
                                        eq = chunks(e[:, 0:L])
                                        dve.tensor_copy(cdec[:, d, :].unsqueeze(2), eq[:, :, P - 1:P] if d == 0 else eq[:, :, 0:1])
                                        dve.tensor_tensor(s_[:, :], e[:, 0:L], q[:, :], ALU.mult)
                                        dve.tensor_tensor(e[:, L:2 * L], e[:, L:2 * L], k_[:, :], ALU.mult).then_inc(mul_done, 1)
                                    elif j == 11:
                                        dve.tensor_tensor(e[:, 0:L], e[:, 0:L], rq[:, :], ALU.mult)
                                        dve.tensor_tensor(e[:, L:2 * L], e[:, L:2 * L], rq[:, :], ALU.mult).then_inc(mul_done, 1)
                                elif name.startswith("post"):
                                    j = int(name[4:])
                                    if j > 1:
                                        dve.drain()
                                    if j == 1:
                                        dve.tensor_copy(att[:, :], at("job1")).then_inc(free[where["job1"][0]], 1)
                                    else:
                                        mask = masks[:, (j - 1) * P:j * P].unsqueeze(1).to_broadcast([P, NT, P])
                                        dve.copy_predicated(chunks(att[:, :]), mask, chunks(at(f"job{j}"))).then_inc(free[where[f"job{j}"][0]], 1)
                                elif step == "rk.d":
                                    rope(h, "rk", rk, 1.0, rk_ready)
                                elif step == "rq.d":
                                    rope(h, "rq", rq, QSCALE, rq_ready)
                                elif step == "KVc":
                                    wait_full(dve, step, h)
                                    dve.tensor_copy(Sf[:, 0, :], at(step)[:, 0:P])
                                    dve.tensor_copy(Sb[:, NT - 1, :], at(step)[:, P:2 * P]).then_inc(free[where[step][0]], 1)
                                elif step in ("KVf", "KVb"):
                                    f = step == "KVf"
                                    S, d = (Sf, 0) if f else (Sb, 1)
                                    for i in range(3):
                                        c, n = (i, i + 1) if f else (3 - i, 2 - i)
                                        dve.drain()
                                        if i == 0:
                                            wait_full(dve, step, h)
                                        m = dve.scalar_tensor_tensor(out=S[:, n, :], in0=S[:, c, :], scalar=cdec[:, d, c:c + 1],
                                                                     in1=at(step)[:, i * P:(i + 1) * P], op0=ALU.mult, op1=ALU.add)
                                    m.then_inc(free[where[step][0]], 1)
                                elif name.startswith("att"):
                                    i = int(name[3:])
                                    wait_full(dve, name, h)
                                    if i == 0:
                                        dve.wait_ge(strip_exp, h + 1)
                                        dve.tensor_tensor(strip[:, 3 * P:4 * P], strip[:, 3 * P:4 * P], ident[:, :], ALU.add)
                                        dve.drain()
                                    if i >= 2:
                                        dve.wait_ge(rav_done, h * 4 + (i - 1))
                                    o = (3 - i) * P
                                    dve.tensor_tensor(ratt[i % 2][:, :], at(name), strip[:, o:o + L], ALU.mult).then_inc(free[where[name][0]], 1)
                                elif step == "rvar":
                                    wait_full(dve, "rmean", h)
                                    for e in range(2):
                                        m = dve.scalar_tensor_tensor(out=ratt[e][:, :], in0=at("rmean"), scalar=-1.0 / (2 * P), in1=ratt[e][:, :],
                                                                     op0=ALU.mult, op1=ALU.add)
                                    m.then_inc(free[where["rmean"][0]], 1)
                                elif step == "hnorm":
                                    dve.wait_ge(hrs_ready, h + 1)
                                    dve.tensor_tensor(q[:, :], at("ho"), kb[:, :], ALU.mult).then_inc(free[5], 1)
                                    dve.drain()
                                    dve.scalar_tensor_tensor(out=q[:, :], in0=q[:, :], scalar=hp[:, HGN:HGN + 1], in1=gate[2][:, :],
                                                             op0=ALU.mult, op1=ALU.mult)
                                    dve.drain()
                                    dve.tensor_copy(y[0][:, 0, :], q[:, :])
                                    dve.drain()
                                    dve.tensor_tensor(y[1][:, 0, :], q[:, :], y[0][:, 0, :].bitcast(F32), ALU.subtract).then_inc(hy_done, 1)
                                elif step == "rnorm":
                                    dve.wait_ge(rrs_ready, h + 1)
                                    for e in range(2):
                                        dve.tensor_tensor(ratt[e][:, :], ratt[e][:, :], rq[:, :], ALU.mult)
                                    dve.drain()
                                    for e in range(2):
                                        dve.tensor_tensor(ratt[e][:, :], ratt[e][:, :], gate[e][:, :], ALU.mult)
                                    dve.drain()
                                    for e in range(2):
                                        dve.tensor_copy(y[0][:, 1 + e, :], ratt[e][:, :])
                                    dve.drain()
                                    for e in range(2):
                                        m = dve.tensor_tensor(y[1][:, 1 + e, :], ratt[e][:, :], y[0][:, 1 + e, :].bitcast(F32), ALU.subtract)
                                    m.then_inc(ry_done, 1)
                                elif step == "pa":
                                    accumulate(h, "pa", range(8), acc[0])
                                elif step == "pb":
                                    accumulate(h, "pb", range(8), acc[1])

        tail = top
        full, free = tail_full, tail_free
        x1 = sb(tail, "x1", [P, KT, L])
        sqsum, sq, sc2 = sb(tail, "sqsum", [P, L]), sb(tail, "sq", [P, L]), sb(tail, "sc2", [P, KT])
        nt = [sb(tail, f"nt{i}", [P, L]) for i in range(2)]
        nu = [sb(tail, f"nu{i}", [P, L]) for i in range(2)]
        sg = nt + nu
        with ExitStack() as st:
            mrg = [sb(st, n, [P, KT, L], F32R) for n in ("mrg_hi", "mrg_lo")]
            xt2 = sb(st, "xt2", [P, NT, D])
        g = [sb(tail, n, [P, FT, L], F32R) for n in ("g_hi", "g_lo")]

        S0, HALF0 = H * NSLAB, H * NSLAB // 2
        SW = S0 + 2 * KT
        SF = SW + KT
        SD = SF + 2 * FT
        BEFORE_DOWN = [4 + FT // 2] * 4 + [6, 6, 3, 2]

        def product(pe, b, n_before, s, slot, pair):
            pe.wait_ge(lo_done, s + 3)
            after(pe, free[b], n_before)
            for k in range(KT):
                m = passes(pe, bank(b), slot, k * P, pair, lambda t: t[:, k, :], k == 0, k == KT - 1)
            m.then_inc(full[b], 1)

        def one(t, n):
            return t[:, bass.ds(n, 1), :].rearrange("p a n -> p (a n)")

        with nc.Block() as block:
            @block.sync
            def _(sp):
                sp.dma_start(xt2[:, :, :], x_dram).then_inc(xt2_in, 16)
                w_out, w_gate, w_up, w_down = (a[n].rearrange("a (k p) n -> p (a k) n", p=P)
                                               for n in ("w_out", "w_ffn_gate", "w_ffn_up", "w_ffn_down"))

                def gate_slab(i, j):
                    col = (COL["ga"] if j < 2 else COL["gb"]) + (j % 2) * P
                    cols = slice(col, col + P) if isinstance(i, int) else bass.ds(i * (2 * P) + col, P)
                    load_slab(sp, j % 2, w_in[:, :, cols], P, i * 4 + (S0 + j))

                for j in (2, 3):
                    gate_slab(0, j)
                with sp.Fori(1, 4) as i:
                    for j in range(4):
                        gate_slab(i, j)
                with sp.Fori(0, 4) as i:
                    for j in range(2):
                        load_slab(sp, j, w_out[:, :, bass.ds(i * (2 * P) + j * P, P)], P, i * 2 + (SW + j))
                with sp.Fori(0, FT // 2) as i:
                    for j in range(4):
                        load_slab(sp, j % 2, (w_up if j % 2 else w_gate)[:, :, bass.ds(i * (2 * P) + (j // 2) * P, P)], P, i * 4 + (SF + j))
                with sp.Fori(0, FT // 2) as i:
                    for j in range(2):
                        load_slab(sp, j, w_down[:, bass.ds(i * 2 + j, 1), :], D, i * 2 + (SD + j))
                for t in range(NT):
                    for c in y_copied:
                        sp.wait_ge(c, t + 1)
                    sp.dma_start(out[0, t * P:(t + 1) * P, :], raw[t % 2][:, :]).then_inc(y_stored[t % 2], 16)
                for done in y_stored:
                    sp.wait_ge(done, 16 * NT // 2)

            @block.gpsimd
            def _(pool):
                with pool.Fori(0, (SD + FT - S0 - 2) // 2) as i:
                    for slot in range(2):
                        split_lo(pool, i * 2 + (S0 + 2 + slot), slot)

            @block.tensor
            def _(pe):
                pe.wait_ge(xt2_in, 16)
                for k in range(KT):
                    b = 4 + k % 4
                    if k >= 4:
                        after(pe, free[b], 1)
                    for t in range(NT):
                        m = pe.transpose(bank(b)[:, t * P:(t + 1) * P], xt2[:, t, k * P:(k + 1) * P], ident[:, :])
                    m.then_inc(full[b], 1)
                with pe.Fori(0, 4) as i:
                    for j in range(4):
                        product(pe, j, i, i * 4 + (S0 + j), j % 2, hx)
                after(pe, mrg_done, KT)
                with pe.Fori(0, 4) as i:
                    for j in range(2):
                        product(pe, 4 + j, i + 2, i * 2 + (SW + j), j, mrg)
                after(pe, sqsum_done, KT)
                after(pe, free[6], 2)
                pe.matmul(bank(6), ones[:, 0:P], sqsum[:, :], start=True, stop=True).then_inc(full[6], 1)
                pe.wait_ge(hx2_ready, KT)
                with pe.Fori(0, FT // 2) as i:
                    for j in range(4):
                        product(pe, j, i + 4, i * 4 + (SF + j), j % 2, hx)

                def down(k, slot, first_, last):
                    pe.wait_ge(lo_done, k + (SD + 3))
                    after(pe, g_done, k + 1)
                    for n in range(KT):
                        if first_:
                            after(pe, free[n], BEFORE_DOWN[n])
                        m = passes(pe, bank(n), slot, n * P, g, lambda t: t[:, k, :] if isinstance(k, int) else one(t, k), first_, last)
                        if last:
                            m.then_inc(full[n], 1)
                    if not last:
                        m.then_inc(down_used, 1)

                for k in range(2):
                    down(k, k, k == 0, False)
                with pe.Fori(1, FT // 2 - 1) as i:
                    for j in range(2):
                        down(i * 2 + j, j, False, False)
                for k in range(FT - 2, FT):
                    down(k, k % 2, False, k == FT - 1)
                after(pe, sqsum_done, 2 * KT)
                after(pe, free[0], BEFORE_DOWN[0] + 1)
                pe.matmul(bank(0), ones[:, 0:P], sqsum[:, :], start=True, stop=True).then_inc(full[0], 1)
                pe.wait_ge(fin_ready, KT)
                for t in range(NT):
                    for half in range(2):
                        b = (2 * t + half + 1) % 8
                        after(pe, free[b], BEFORE_DOWN[b] + (2 if b == 0 else 1))
                        for k in range(4):
                            m = pe.transpose(bank(b)[:, k * P:(k + 1) * P], x1[:, 4 * half + k, t * P:(t + 1) * P], ident[:, :])
                        m.then_inc(full[b], 1)

            @block.scalar
            def _(act):
                for k in range(KT):
                    b = 4 + k % 4
                    act.wait_ge(full[b], k // 4 + 1)
                    act.activation(x1[:, k, :], bank(b), ACT.Copy).then_inc(free[b], 1)
                with act.Fori(0, 4) as i:
                    for j in range(4):
                        act.wait_ge(full[j], i + 1)
                        if j % 2 == 0:
                            after(act, mrg_done, i * 2)
                        act.activation(sg[j][:, :], bank(j), ACT.Sigmoid).then_inc(free[j], 1)
                        split_hi(act, i * 2 + (HALF0 + j // 2 + 1), j % 2)
                with act.Fori(0, 4) as i:
                    for j in range(2):
                        act.wait_ge(full[4 + j], i + 3)
                        split_hi(act, i + (HALF0 + 9), j)
                        after(act, free[4 + j], i + 3)
                        after(act, sqsum_done, i * 2 + j)
                        act.activation(sq[:, :], one(x1, i * 2 + j), ACT.Square).then_inc(sq_ready, 1)

                def rstd(b, n):
                    act.wait_ge(full[b], n)
                    act.activation(sqsum[:, :], bank(b), ACT.Ln, bias=eps[:, 0:1], scale=1.0 / D).then_inc(free[b], 1)
                    act.drain()
                    act.activation(sqsum[:, :], sqsum[:, :], ACT.Exp, scale=-0.5).then_inc(tail_rstd, 1)

                rstd(6, 3)
                act.wait_ge(mod_ready, 1)
                for k in range(KT):
                    act.wait_ge(nt_ready, k + 1)
                    if k >= 2:
                        act.wait_ge(hx2_ready, k - 1)
                    act.activation(nu[k % 2][:, :], nt[k % 2][:, :], ACT.Identity, bias=modt[:, 24 + k, 0:1], scale=sc2[:, k:k + 1]).then_inc(nu_ready, 1)
                with act.Fori(0, FT // 2) as i:
                    for j in range(4):
                        act.wait_ge(full[j], i + 5)
                        if j % 2 == 0:
                            after(act, g_done, i * 2)
                            act.wait_ge(hx2_ready, KT)
                            act.activation(nt[j // 2][:, :], bank(j), ACT.Silu).then_inc(free[j], 1)
                        split_hi(act, i * 2 + (HALF0 + 12 + j // 2 + 1), j % 2)
                with act.Fori(0, FT // 2 - 1) as i:
                    for j in range(2):
                        act.wait_ge(down_used, i * 2 + (j + 1))
                        split_hi(act, i + (HALF0 + 12 + FT + 1), j)
                for n in range(KT):
                    after(act, free[n], BEFORE_DOWN[n] + 1)
                    after(act, sqsum_done, KT + n)
                    act.activation(sq[:, :], x1[:, n, :], ACT.Square).then_inc(sq_ready, 1)
                rstd(0, BEFORE_DOWN[0] + 2)
                for t in range(NT):
                    b = (2 * t + 1) % 8
                    act.wait_ge(full[b], BEFORE_DOWN[b] + 2)
                    if t >= 2:
                        act.wait_ge(y_stored[t % 2], 16 * (t // 2))
                    act.activation(raw[t % 2][:, 0:512], bank(b), ACT.Copy).then_inc(y_copied[0], 1)

            @block.vector
            def _(dve):
                dve.tensor_tensor(modt[:, 16:48, 0], modt[:, 16:48, 0], chan[:, PBM + 16:PBM + 48], ALU.add)
                dve.drain()
                dve.scalar_tensor_tensor(out=sc2[:, :], in0=modt[:, 32:40, 0], scalar=1.0, in1=chan[:, PN2:PN2 + 8],
                                         op0=ALU.add, op1=ALU.mult).then_inc(mod_ready, 1)
                dve.memset(sqsum[:, :], 0.0)
                with dve.Fori(0, 4) as i:
                    for j in range(2):
                        n = i * 2 + j
                        after(dve, free[j], i + 1)
                        dve.tensor_tensor(sg[j][:, :], sg[j][:, :], one(acc[0], n), ALU.mult)
                        after(dve, free[2 + j], i + 1)
                        dve.tensor_tensor(sg[2 + j][:, :], sg[2 + j][:, :], one(acc[1], n), ALU.mult)
                        dve.drain()
                        dve.tensor_tensor(sg[j][:, :], sg[j][:, :], sg[2 + j][:, :], ALU.add)
                        dve.drain()
                        dve.tensor_copy(one(mrg[0], n), sg[j][:, :])
                        dve.drain()
                        dve.tensor_tensor(one(mrg[1], n), sg[j][:, :], one(mrg[0], n).bitcast(F32), ALU.subtract).then_inc(mrg_done, 1)
                after(dve, free[7], 2)
                with dve.Fori(0, 4) as i:
                    for j in range(2):
                        n = i * 2 + j
                        dve.wait_ge(full[4 + j], i + 3)
                        g1 = modt[:, bass.ds(i * 2 + (16 + j), 1), 0:1].rearrange("p a c -> p (a c)")
                        dve.scalar_tensor_tensor(out=one(x1, n), in0=bank(4 + j), scalar=g1, in1=one(x1, n),
                                                 op0=ALU.mult, op1=ALU.add).then_inc(free[4 + j], 1)
                        dve.wait_ge(sq_ready, i * 2 + (j + 1))
                        dve.tensor_tensor(sqsum[:, :], sqsum[:, :], sq[:, :], ALU.add).then_inc(sqsum_done, 1)
                dve.wait_ge(tail_rstd, 1)

                def split_hx(k):
                    dve.wait_ge(nu_ready, k + 1)
                    dve.tensor_copy(hx[0][:, k, :], nu[k % 2][:, :])
                    dve.drain()
                    dve.tensor_tensor(hx[1][:, k, :], nu[k % 2][:, :], hx[0][:, k, :].bitcast(F32), ALU.subtract).then_inc(hx2_ready, 1)

                for k in range(KT):
                    dve.tensor_tensor(nt[k % 2][:, :], x1[:, k, :], sqsum[:, :], ALU.mult).then_inc(nt_ready, 1)
                    if k >= 1:
                        split_hx(k - 1)
                split_hx(KT - 1)
                dve.drain()
                dve.memset(sqsum[:, :], 0.0)
                with dve.Fori(0, FT // 2) as i:
                    for t in range(2):
                        n = i * 2 + t
                        after(dve, free[2 * t], i + 5)
                        dve.wait_ge(full[2 * t + 1], i + 5)
                        dve.tensor_tensor(nu[t][:, :], bank(2 * t + 1), nt[t][:, :], ALU.mult).then_inc(free[2 * t + 1], 1)
                        dve.drain()
                        dve.tensor_copy(one(g[0], n), nu[t][:, :])
                        dve.drain()
                        dve.tensor_tensor(one(g[1], n), nu[t][:, :], one(g[0], n).bitcast(F32), ALU.subtract).then_inc(g_done, 1)
                for n in range(KT):
                    dve.wait_ge(full[n], BEFORE_DOWN[n] + 1)
                    dve.scalar_tensor_tensor(out=x1[:, n, :], in0=bank(n), scalar=modt[:, 40 + n, 0:1], in1=x1[:, n, :],
                                             op0=ALU.mult, op1=ALU.add).then_inc(free[n], 1)
                    if n >= 1:
                        dve.wait_ge(sq_ready, KT + n)
                        dve.tensor_tensor(sqsum[:, :], sqsum[:, :], sq[:, :], ALU.add).then_inc(sqsum_done, 1)
                        dve.drain()
                dve.wait_ge(sq_ready, 2 * KT)
                dve.tensor_tensor(sqsum[:, :], sqsum[:, :], sq[:, :], ALU.add).then_inc(sqsum_done, 1)
                dve.wait_ge(tail_rstd, 2)
                for n in range(KT):
                    dve.scalar_tensor_tensor(out=x1[:, n, :], in0=x1[:, n, :], scalar=chan[:, PFN + n:PFN + n + 1], in1=sqsum[:, :],
                                             op0=ALU.mult, op1=ALU.mult).then_inc(fin_ready, 1)
                for t in range(NT):
                    b = (2 * t + 2) % 8
                    dve.wait_ge(full[b], BEFORE_DOWN[b] + (3 if b == 0 else 2))
                    if t >= 2:
                        dve.wait_ge(y_stored[t % 2], 16 * (t // 2))
                    dve.tensor_copy(raw[t % 2][:, 512:1024], bank(b)).then_inc(y_copied[1], 1)


_INS = ["x", "c", "ctx", "c_ctx", "w_mod", "b_mod", "norm1_w", "norm2_w", "w_in", "hg_lb_fwd", "hg_lb_bwd", "hg_norm_w",
        "rt_theta_fwd", "rt_theta_bwd", "w_proj_hgrn", "w_proj_ret", "w_out", "w_ffn_gate", "w_ffn_up", "w_ffn_down", "final_norm_w"]


def kernel(**inputs):
    import numpy as _np
    import concourse.bacc as _bacc
    from concourse import mybir as _mybir
    from concourse.bass_utils import run_bass_kernel_spmd as _run

    nc = _bacc.Bacc("TRN2", target_bir_lowering=False, num_devices=1)
    arrays, aps = {}, {}
    host = {n: _np.ascontiguousarray(inputs[n]) for n in _INS}
    host.update(constants())
    for name, arr in host.items():
        arrays[f"in_{name}_dram"] = arr
        aps[name] = nc.dram_tensor(f"in_{name}_dram", arr.shape, _mybir.dt.from_np(arr.dtype), kind="ExternalInput").ap()
    out = nc.dram_tensor("out_0_dram", (1, L, D), F32, kind="ExternalOutput").ap()
    build(nc, aps, out)
    r = _run(nc, [arrays], core_ids=[0])
    return r.results[0]["out_0_dram"]
```

```python
from contextlib import ExitStack

import numpy as np
import concourse.bass as bass
from concourse import mybir

F32 = mybir.dt.float32
F32R = mybir.dt.float32r
F16 = mybir.dt.float16
U8 = mybir.dt.uint8
ACT = mybir.ActivationFunctionType
ALU = mybir.AluOpType

P = 128
D = 1024
KT = D // P
L = 512
LC = 256
NT, NC = L // P, LC // P
H = 8
DK = 128
GRID_W = 64
D_FF = 2816
FT = D_FF // P
EPS, GN_EPS = 1e-6, 1e-5
QSCALE = DK ** -0.5

COL = dict(hq=0, hf_f=1024, hf_b=2048, hi=3072, hg=4096, rq=5120, rk=6144, rv=7168, rg=9216, ga=11264, gb=12288)

PC, PCC, PN1, PN2, PFN, PHG, PLF, PLB, PBM = 0, 8, 16, 24, 32, 40, 48, 64, 80
LBF, OMF, LBB, OMB, HGN, LGF, LGB, WC = 0, 1, 2, 3, 4, 5, 6, 7
HPN = 11

SLABS = {
    "rg0": (COL["rg"], 256, 0, False), "rg1": (COL["rg"], 256, 1, False), "g": (COL["hg"], 128, 0, False),
    "f": (COL["hf_f"], 128, 0, True), "b": (COL["hf_b"], 128, 0, True), "q": (COL["hq"], 128, 0, False),
    "v": (COL["hi"], 128, 0, True), "rk": (COL["rk"], 128, 0, True), "rv0": (COL["rv"], 256, 0, True),
    "rv1": (COL["rv"], 256, 1, True), "rq": (COL["rq"], 128, 0, False),
}
PROJ = {"pa": range(8), "pb0": range(4), "pb1": range(4, 8)}
NSLAB = len(SLABS) + len(PROJ)
HALVES = [64, 32, 16, 8, 4, 2, 1]
MOD_AFTER = {"q": 0, "rg0": 1, "rq": 2, "g": 3}
STEPS = [
    "f.a", "hstat'", "rmean'", "f.b", "rcent'", "f.d", "f.c", "f.e", "rvar'",
    "b.a", "b.b", "b.d", "b.c", "b.e", "hgn'", "hp", "lns'", "gates", "norms'",
    "q.a", "q.b", "q.d", "v.a", "v.b", "v.d", "v.c", "v.e", "prep0",
    "rk.a", "Tv", "prep1", "mul0", "rk.b", "mod0", "rk.d", "rk.c", "rk.e", "job0", "mul1", "pa.0'", "pa.1'", "pa.2'", "pa.3'", "prep2",
    "job1", "KVc", "pb0.0'", "mul2", "pb0.1'", "prep3", "post1", "rv0.a", "job2", "prep4", "mul3", "post2", "strip",
    "rv0.b", "rv0.d", "rv0.c", "rv0.e",
    "job3", "pb1.0'", "prep5", "mul4", "pb1.1'", "post3", "Trv0", "rg0.a", "job4", "prep6", "mul5", "post4", "rg0.b", "rg0.d", "mod1",
    "job5", "prep7", "mul6", "post5", "rv1.a", "rv1.b", "rv1.d", "rv1.c", "rv1.e", "job6", "mul7",
    "rq.a", "job7", "mul8", "post6", "prep9", "post7", "rq.b", "rq.d", "Trv1", "rg1.a", "job8", "mod2", "prep10", "mul9", "post8",
    "rg1.b", "rg1.d", "job9", "prep11", "rkT", "mul10", "mul11", "g.a", "job10", "g.b", "KVf", "rKV", "g.d",
    "att0", "KVb", "att1", "av0", "att2", "av1", "att3", "av2", "hgo", "av3", "mod3", "rstate",
]
PHASES = {
    "first": [s for s in STEPS if s[-1] != "'"],
    "loop": STEPS,
    "last": [s for s in STEPS if s[-1] == "'"],
}


def tiles_of(name, part):
    return PROJ[name][2 * int(part):2 * int(part) + 2]


def bank_uses():
    def uses(step):
        name, _, part = step.rstrip("'").partition(".")
        if part == "a":
            return [(name, "gemm")]
        if part == "c":
            return [(name + ".ctx", 2)]
        if name[:3] == "mod":
            return [(name + ".ctx", 2)]
        if name in PROJ:
            return [(f"{name[:2]}{n}", "gemm") for n in tiles_of(name, part)]
        if name in ("Tv", "Trv0", "Trv1"):
            return [(name, "mix"), (name + "c", 2)]
        if name == "hstat":
            return [(name, 7)]
        if name[:3] in ("job", "KVc", "KVf", "KVb", "rkT", "rKV", "att") or name in ("rmean", "rvar"):
            return [(name, "mix")]
        return {"hgo": [("ho", 5)], "rstate": [("ro0", 6), ("ro1", 7)]}.get(name, [])

    bank, late, n_of = {}, set(), {"gemm": 0, "mix": 0}
    for step in STEPS:
        for name, kind in uses(step):
            if kind in n_of:
                bank[name] = (0 if kind == "gemm" else 3) + n_of[kind] % 2
                n_of[kind] += 1
            else:
                bank[name] = kind
            if step[-1] == "'":
                late.add(name)
    per = {b: sum(x == b for x in bank.values()) for b in range(8)}
    place = {}
    for phase, steps in PHASES.items():
        n = {b: 0 if phase == "first" else -sum(bank[x] == b for x in late) for b in range(8)}
        place[phase] = {x: place["loop"][x] for x in ("ho", "ro0", "ro1")} if phase == "last" else {}
        for step in steps:
            for name, _ in uses(step):
                place[phase][name] = n[bank[name]] + (per[bank[name]] if name in late else 0)
                n[bank[name]] += 1
    return bank, place, per


def slab_order():
    order = {}
    for phase, steps in PHASES.items():
        n = 0 if phase == "first" else -len(PROJ)
        order[phase] = {}
        for step in steps:
            name, _, part = step.rstrip("'").partition(".")
            if part == "a" or (name in PROJ and part == "0"):
                order[phase][name] = n
                n += 1
    return order


def constants():
    t = np.arange(P)
    masks = []
    for h in HALVES:
        same = (t[:, None] // (2 * h)) == (t[None, :] // (2 * h))
        masks.append(same & ((t[:, None] // h) != (t[None, :] // h)))
    masks.append(np.eye(P, dtype=bool))
    n_f = DK // 4
    freqs = np.float32(10000.0) ** (-np.arange(n_f, dtype=np.float32) / np.float32(n_f))
    pos = np.arange(L)
    row, col = (pos // GRID_W).astype(np.float32), (pos % GRID_W).astype(np.float32)
    ang = np.concatenate([row[:, None] * freqs, col[:, None] * freqs], axis=-1).astype(np.float32)
    cos, sin = np.cos(ang).T.astype(np.float32), np.sin(ang).T.astype(np.float32)
    u = np.arange(7 * P)[None, :] - 3 * P - t[:, None]
    s = np.arange(LC).reshape(NC, P).T
    return {
        "k_ident": np.eye(P, dtype=np.float32),
        "k_masks": np.stack(masks, axis=1).reshape(P, 8 * P).astype(np.float32),
        "k_first": np.tile((pos % P != 0).astype(np.float32), (P, 1)),
        "k_cos": np.concatenate([cos, cos], axis=0),
        "k_sin": np.concatenate([sin, -sin], axis=0),
        "k_upos": np.maximum(u, 0).astype(np.float16),
        "k_uneg": np.maximum(-u, 0).astype(np.float16),
        "k_tpos": np.tile((pos + 1).astype(np.float16), (P, 1)),
        "k_spos": np.concatenate([LC - 1 - s, s], axis=1).astype(np.float32),
    }


def build(nc, a, out):
    bank_of, places, per = bank_uses()
    slabs = slab_order()
    with ExitStack() as top:
        def sem(name):
            return top.enter_context(nc.semaphore(name))

        begun = []

        def sem_from_1(name):
            begun.append(sem(name))
            return begun[-1]

        def after(eng, s, n):
            eng.wait_ge(s, n + 1)

        def sb(stack, name, shape, dt=F32):
            return stack.enter_context(nc.sbuf_tensor(name, shape, dt))

        psum = [top.enter_context(nc.psum_tensor(f"bank{i}", [P, 512], F32)) for i in range(8)]

        def bank(i):
            return psum[i][:, :]

        def at(name):
            return bank(bank_of[name])[:, 0:LC if name.endswith(".ctx") else L]

        ident = sb(top, "ident", [P, P])
        ones = sb(top, "ones", [P, 256])
        chan = sb(top, "chan", [P, P])
        heads = sb(top, "heads", [P, H, HPN])
        modt = sb(top, "modt", [P, 48, 2])
        eps = sb(top, "eps", [P, 2])
        silu_c = sb(top, "silu_c", [P, 16])
        silu_k = silu_c[:, :].rearrange("p (c k) -> p k c", k=KT)
        hx = [sb(top, n, [P, KT, L], F32R) for n in ("hx_hi", "hx_lo")]
        raw = [sb(top, f"raw{i}", [P, D]) for i in range(2)]
        whi = [sb(top, f"whi{i}", [P, D], F32R) for i in range(2)]
        wlo = [sb(top, f"wlo{i}", [P, D], F32R) for i in range(2)]
        acc = [sb(top, n, [P, KT, L]) for n in ("acc_a", "acc_b")]

        w_landed = [sem("w_landed0"), sem("w_landed1")]
        hi_done = sem("hi_done")
        lo_done = sem("lo_done")

        w_in = a["w_in"].rearrange("a (k p) n -> p (a k) n", p=P)
        x_dram = a["x"].rearrange("a (t p) d -> p (a t) d", p=P)
        ctx_dram = a["ctx"].rearrange("a (t p) d -> p (a t) d", p=P)
        wmod = a["w_mod"].rearrange("a (k p) n -> p (a k) n", p=P)

        def kp(tile, n=P):
            return tile[:, :].rearrange("p (k n) -> p k n", n=n)

        def load_slab(sp, slot, src, n, s):
            if s is not None:
                sp.wait_ge(lo_done, s + 1)
            sp.dma_start(kp(raw[slot], n), src).then_inc(w_landed[slot], 16)

        def split_hi(act, half, slot):
            act.wait_ge(w_landed[slot], half * 16 + 16)
            act.activation(whi[slot][:, :], raw[slot][:, :], ACT.Copy).then_inc(hi_done, 1)

        def split_lo(pool, s, slot):
            pool.wait_ge(hi_done, s + 1)
            pool.tensor_tensor(wlo[slot][:, :], raw[slot][:, :], whi[slot][:, :].bitcast(F32),
                               ALU.subtract).then_inc(lo_done, 1)

        def passes(pe, dst, slot, col, pair, pick, start, stop):
            cols = slice(col, col + P)
            pe.matmul(dst, whi[slot][:, cols], pick(pair[0]), start=start, stop=False)
            pe.matmul(dst, whi[slot][:, cols], pick(pair[1]), start=False, stop=False)
            return pe.matmul(dst, wlo[slot][:, cols], pick(pair[0]), start=False, stop=stop)

        full = [sem(f"full{i}") for i in range(8)]
        free = [sem_from_1(f"free{i}") for i in range(8)]
        mraw_in, mraw_summed, mraw_used = sem("mraw_in"), sem("mraw_summed"), sem_from_1("mraw_used")
        hp_ready = sem("hp_ready")
        ln_ready = sem("ln_ready")
        args_ready, exp_done, mul_done = sem("args_ready"), sem("exp_done"), sem("mul_done")
        rk_ready, rq_ready = sem("rk_ready"), sem("rq_ready")
        strip_arg, strip_exp = sem("strip_arg"), sem("strip_exp")
        rav_done = sem("rav_done")
        hsq_ready, hrs_ready, hy_done = sem("hsq_ready"), sem("hrs_ready"), sem("hy_done")
        rsum_ready = sem("rsum_ready")
        rsq_ready, rrs_ready, ry_done = sem("rsq_ready"), sem("rrs_ready"), sem("ry_done")
        tail_full = [sem(f"tail_full{i}") for i in range(8)]
        tail_free = [sem_from_1(f"tail_free{i}") for i in range(8)]
        xt2_in, mod_ready, mrg_done = sem("xt2_in"), sem("mod_ready"), sem_from_1("mrg_done")
        sq_ready, sqsum_done, tail_rstd = sem("sq_ready"), sem_from_1("sqsum_done"), sem("tail_rstd")
        sq_summed = sem("sq_summed")
        nt_ready, nu_ready, hx2_ready = sem("nt_ready"), sem("nu_ready"), sem("hx2_ready")
        g_done, down_used, fin_ready = sem_from_1("g_done"), sem("down_used"), sem("fin_ready")
        y_copied, y_stored = [sem("y_copied_act"), sem("y_copied_dve")], sem("y_stored")

        with ExitStack() as main:
            hc = [sb(main, n, [P, KT, LC], F32R) for n in ("hc_hi", "hc_lo")]
            masks = sb(main, "masks", [P, 8 * P], U8)
            first = sb(main, "first", [P, L])
            cosT = sb(main, "cosT", [P, L])
            sinT = sb(main, "sinT", [P, L])
            upos = sb(main, "upos", [P, 7 * P], F16)
            uneg = sb(main, "uneg", [P, 7 * P], F16)
            tpos = sb(main, "tpos", [P, L], F16)

            with ExitStack() as st:
                xt = sb(st, "xt", [P, NT + NC, D])
                wm = [sb(st, f"wm{i}", [P, KT, 512]) for i in range(2)]
                rows = sb(st, "rows", [P, P])
                theta = sb(st, "theta", [P, 16])
                tmp = [sb(st, f"ttmp{i}", [P, 16]) for i in range(4)]
                spos = sb(st, "spos", [P, 4])
                ss = sb(st, "ss", [P, 8])
                rstd = sb(st, "rstd", [P, 8])
                junk = sb(st, "junk", [P, D])
                masks_f = sb(st, "masks_f", [P, 8 * P])
                sc1 = sb(st, "sc1", [P, KT, 2])
                u = [sb(st, f"u{i}", [P, L + LC]) for i in range(2)]
                mod_rows = sb(st, "mod_rows", [2, 2 * D])
                MOD_BANK = (1, 6, 7, 0)
                rows_in, const_in, x_in = sem("rows_in"), sem("const_in"), sem("x_in")
                wm_in = [sem("wm_in0"), sem("wm_in1")]
                wm_used, rows_t, chan_ready, silu_ready = sem("wm_used"), sem("rows_t"), sem("chan_ready"), sem("silu_ready")
                mod_ps, mod_done, sc_ready = sem("mod_ps"), sem("mod_done"), sem("sc_ready")
                ss_ready, rstd_ready, xn_ready = sem("ss_ready"), sem("rstd_ready"), sem("xn_ready")
                tx_full, tx_free, u_split, u_split_lo = sem("tx_full"), sem("tx_free"), sem("u_split"), sem("u_split_lo")
                th_ready, th_exp, th_ln, eps_ready, hx_hi_done, lg_ready = (sem("th_ready"), sem("th_exp"), sem("th_ln"), sem("eps_ready"),
                                                                  sem("hx_hi_done"), sem("lg_ready"))
                lbs, slots_ready = sem("lbs"), sem("slots_ready")
                wctx_done = sem("wctx_done")

                with nc.Block() as block:
                    @block.sync
                    def _(sp):
                        def row(lo, n, src):
                            sp.dma_start(rows[lo:lo + n, :], src).then_inc(rows_in, 16)
                        row(PC, 8, a["c"].rearrange("a (k p) -> (a k) p", p=P))
                        row(PCC, 8, a["c_ctx"].rearrange("(k p) -> k p", p=P))
                        row(PN1, 8, a["norm1_w"].rearrange("a (k p) -> (a k) p", p=P))
                        row(PN2, 8, a["norm2_w"].rearrange("a (k p) -> (a k) p", p=P))
                        row(PFN, 8, a["final_norm_w"].rearrange("(k p) -> k p", p=P))
                        row(PHG, 8, a["hg_norm_w"].rearrange("a (k p) -> (a k) p", p=P))
                        row(PLF, 16, a["hg_lb_fwd"].rearrange("a (k p) -> (a k) p", p=P))
                        row(PLB, 16, a["hg_lb_bwd"].rearrange("a (k p) -> (a k) p", p=P))
                        row(PBM, 48, a["b_mod"].rearrange("a (k p) -> (a k) p", p=P))
                        for dst, src in ((ident, "k_ident"), (spos, "k_spos")):
                            sp.dma_start(dst[:, :], a[src]).then_inc(const_in, 16)
                        sp.dma_start(theta[:, 0:8], a["rt_theta_fwd"].to_broadcast([P, 8])).then_inc(const_in, 16)
                        sp.dma_start(theta[:, 8:16], a["rt_theta_bwd"].to_broadcast([P, 8])).then_inc(const_in, 16)
                        sp.dma_start(wm[0][:, :, :], wmod[:, :, 0:512]).then_inc(wm_in[0], 16)
                        sp.dma_start(wm[1][:, :, :], wmod[:, :, 512:1024]).then_inc(wm_in[1], 16)
                        sp.dma_start(xt[:, 0:NT, :], x_dram).then_inc(x_in, 16)
                        sp.dma_start(xt[:, NT:NT + NC, :], ctx_dram).then_inc(x_in, 16)
                        for j in (2, 3):
                            sp.wait_ge(wm_used, j - 1)
                            sp.dma_start(wm[j % 2][:, :, :], wmod[:, :, j * 512:(j + 1) * 512]).then_inc(wm_in[j % 2], 16)
                        for dst, src in ((masks_f, "k_masks"), (first, "k_first"), (cosT, "k_cos"), (sinT, "k_sin"),
                                         (upos, "k_upos"), (uneg, "k_uneg"), (tpos, "k_tpos")):
                            sp.dma_start(dst[:, :], a[src]).then_inc(const_in, 16)
                        for slot in range(2):
                            col, _, tile, _ = SLABS[list(slabs["first"])[slot]]
                            sp.dma_start(kp(raw[slot]), w_in[:, :, col + tile * P:col + (tile + 1) * P]).then_inc(w_landed[slot], 16)
                        sp.wait_ge(const_in, 16 * 11)

                    @block.gpsimd
                    def _(pool):
                        pool.memset(acc[0][:, :, :], 0.0).then_inc(slots_ready, 1)
                        pool.memset(acc[1][:, :, :], 0.0).then_inc(lo_done, 1)
                        pool.memset(ones[:, :], 1.0).then_inc(lo_done, 1)
                        for s in begun:
                            pool.nop().then_inc(s, 1)
                        for slot in range(2):
                            split_lo(pool, slot, slot)
                        for k in range(KT):
                            pool.wait_ge(hx_hi_done, k + 1)
                            pool.tensor_tensor(hx[1][:, k, :], u[k % 2][:, 0:L], hx[0][:, k, :].bitcast(F32), ALU.subtract).then_inc(u_split_lo, 1)

                    @block.tensor
                    def _(pe):
                        pe.wait_ge(rows_in, 16 * 9)
                        pe.wait_ge(const_in, 16 * 4)
                        pe.transpose(psum[0][:, 0:P], rows[:, :], ident[:, :]).then_inc(rows_t, 1)
                        pe.wait_ge(silu_ready, 1)
                        for j in range(4):
                            pe.wait_ge(wm_in[j % 2], 16 * (j // 2 + 1))
                            for k in range(KT):
                                m = pe.matmul(psum[MOD_BANK[j]][0:2, :], silu_k[:, k, :], wm[j % 2][:, k, :], start=(k == 0), stop=(k == KT - 1))
                            m.then_inc(wm_used, 1)
                        pe.wait_ge(xn_ready, NT + NC)
                        for k in range(KT):
                            if k == 2:
                                pe.wait_ge(mod_done, 4)
                                for t in range(16):
                                    m = pe.transpose(psum[1][:, 2 * t:2 * t + 2], mod_rows[0:2, t * P:(t + 1) * P], ident[0:2, 0:2])
                                m.then_inc(mod_ps, 1)
                            b = 2 + 2 * (k % 2)
                            if k >= 2:
                                pe.wait_ge(tx_free, k - 1)
                            for t in range(NT + NC):
                                m = pe.transpose(psum[b + t // 4][:, (t % 4) * P:(t % 4 + 1) * P], xt[:, t, k * P:(k + 1) * P], ident[:, :])
                            m.then_inc(tx_full, 1)

                    @block.scalar
                    def _(act):
                        act.wait_ge(chan_ready, 1)
                        act.activation(silu_c[:, :], chan[:, PC:PC + 16], ACT.Silu).then_inc(silu_ready, 1)
                        act.wait_ge(x_in, 32)
                        for t in range(NT + NC):
                            act.activation(junk[:, :], xt[:, t, :], ACT.Square, accum_out=ss[:, t:t + 1]).then_inc(ss_ready, 1)
                            act.drain()
                        act.wait_ge(eps_ready, 2)
                        act.activation(rstd[:, 0:6], ss[:, 0:6], ACT.Ln, bias=eps[:, 0:1], scale=1.0 / D)
                        act.drain()
                        act.activation(rstd[:, 0:6], rstd[:, 0:6], ACT.Exp, scale=-0.5).then_inc(rstd_ready, 1)
                        act.wait_ge(th_ready, 1)
                        act.activation(tmp[0][:, :], tmp[0][:, :], ACT.Exp, scale=-1.0).then_inc(th_exp, 1)
                        act.wait_ge(th_ready, 2)
                        act.activation(tmp[2][:, :], tmp[1][:, :], ACT.Ln).then_inc(th_ln, 1)
                        act.wait_ge(lg_ready, 1)
                        for h in range(H):
                            act.activation(heads[:, h, WC:WC + 2], spos[:, 0:2], ACT.Exp, scale=heads[:, h, LGF:LGF + 1])
                            act.activation(heads[:, h, WC + 2:WC + 4], spos[:, 2:4], ACT.Exp, scale=heads[:, h, LGB:LGB + 1]).then_inc(wctx_done, 1)
                        act.wait_ge(lbs, 1)
                        for dst, src, sc in ((LBF, 0, 1.0), (OMF, 0, -1.0), (LBB, 1, 1.0), (OMB, 1, -1.0)):
                            act.activation(heads[:, :, dst], tmp[3][:, 8 * src:8 * src + 8], ACT.Sigmoid, scale=sc)
                        for slot in range(2):
                            split_hi(act, 0, slot)
                        act.wait_ge(sc_ready, 1)
                        for k in range(KT):
                            act.wait_ge(tx_full, k + 1)
                            if k >= 2:
                                act.wait_ge(u_split, k - 1)
                                act.wait_ge(u_split_lo, k - 1)
                            b = 2 + 2 * (k % 2)
                            act.activation(u[k % 2][:, 0:L], psum[b][:, :], ACT.Identity, bias=modt[:, k, 0:1], scale=sc1[:, k, 0:1])
                            act.activation(u[k % 2][:, L:L + LC], psum[b + 1][:, 0:LC], ACT.Identity, bias=modt[:, k, 1:2],
                                           scale=sc1[:, k, 1:2]).then_inc(tx_free, 1)

                    @block.vector
                    def _(dve):
                        dve.memset(eps[:, 0:1], EPS).then_inc(eps_ready, 1)
                        dve.memset(eps[:, 1:2], GN_EPS).then_inc(eps_ready, 1)
                        dve.wait_ge(rows_t, 1)
                        dve.tensor_copy(chan[:, :], psum[0][:, 0:P]).then_inc(chan_ready, 1)
                        dve.wait_ge(const_in, 16 * 4)
                        dve.tensor_scalar(tmp[0][:, :], theta[:, :], -80.0, None, ALU.max).then_inc(th_ready, 1)
                        dve.wait_ge(th_exp, 1)
                        dve.tensor_scalar(tmp[1][:, :], tmp[0][:, :], 1.0, None, ALU.add).then_inc(th_ready, 1)
                        dve.wait_ge(th_ln, 1)
                        dve.drain()
                        dve.tensor_scalar(tmp[3][:, :], tmp[1][:, :], -1.0, None, ALU.add)
                        dve.drain()
                        dve.tensor_scalar(tmp[1][:, :], tmp[3][:, :], 0.0, None, ALU.is_equal)
                        dve.drain()
                        dve.tensor_tensor(tmp[3][:, :], tmp[3][:, :], tmp[1][:, :], ALU.add)
                        dve.tensor_tensor(tmp[2][:, :], tmp[2][:, :], tmp[1][:, :], ALU.add)
                        dve.drain()
                        dve.reciprocal(tmp[3][:, :], tmp[3][:, :])
                        dve.tensor_tensor(tmp[2][:, :], tmp[2][:, :], tmp[0][:, :], ALU.mult)
                        dve.drain()
                        dve.tensor_tensor(tmp[2][:, :], tmp[2][:, :], tmp[3][:, :], ALU.mult)
                        dve.drain()
                        for d, dst in ((0, LGF), (1, LGB)):
                            m = dve.tensor_scalar(heads[:, :, dst], tmp[2][:, 8 * d:8 * d + 8], -1.0, None, ALU.mult)
                        m.then_inc(lg_ready, 1)
                        dve.tensor_copy(heads[:, :, HGN], chan[:, PHG:PHG + 8])
                        dve.tensor_tensor(tmp[3][:, 0:8], chan[:, PLF:PLF + 8], chan[:, PLF + 8:PLF + 16], ALU.subtract)
                        dve.tensor_tensor(tmp[3][:, 8:16], chan[:, PLB:PLB + 8], chan[:, PLB + 8:PLB + 16], ALU.subtract).then_inc(lbs, 1)
                        dve.wait_ge(rstd_ready, 1)
                        for t in range(NT + NC):
                            dve.tensor_scalar(xt[:, t, :], xt[:, t, :], rstd[:, t:t + 1], None, ALU.mult).then_inc(xn_ready, 1)
                        for j in range(4):
                            dve.wait_ge(wm_used, j + 1)
                            dve.tensor_copy(mod_rows[0:2, j * 512:(j + 1) * 512], psum[MOD_BANK[j]][0:2, :]).then_inc(mod_done, 1)
                        dve.wait_ge(mod_ps, 1)
                        dve.tensor_tensor(modt[:, 0:16, :], psum[1][:, 0:32].rearrange("p (t c) -> p t c", c=2),
                                          chan[:, PBM:PBM + 16].unsqueeze(2).to_broadcast([P, 16, 2]), ALU.add)
                        dve.drain()
                        dve.scalar_tensor_tensor(out=sc1[:, :, :], in0=modt[:, 8:16, :], scalar=1.0,
                                                 in1=chan[:, PN1:PN1 + 8].unsqueeze(2).to_broadcast([P, 8, 2]),
                                                 op0=ALU.add, op1=ALU.mult).then_inc(sc_ready, 1)
                        for k in range(KT):
                            dve.wait_ge(tx_free, k + 1)
                            dve.tensor_copy(hx[0][:, k, :], u[k % 2][:, 0:L]).then_inc(hx_hi_done, 1)
                            dve.tensor_copy(hc[0][:, k, :], u[k % 2][:, L:L + LC])
                            dve.drain()
                            dve.tensor_tensor(hc[1][:, k, :], u[k % 2][:, L:L + LC], hc[0][:, k, :].bitcast(F32), ALU.subtract).then_inc(u_split, 1)
                        dve.wait_ge(const_in, 16 * 11)
                        dve.tensor_copy(masks[:, :], masks_f[:, :])

            with ExitStack() as st:
                mraw = sb(st, "mraw", [P, KT, P])
                hp = sb(st, "hp", [P, HPN])
                hgn = sb(st, "hgn", [P, 1])
                q, kf, kb, bf, bb = [sb(st, n, [P, L]) for n in ("q", "kf", "kb", "bf", "bb")]
                kfc, kbc, gfc, gbc = [sb(st, n, [P, LC]) for n in ("kfc", "kbc", "gfc", "gbc")]
                vT = sb(st, "vT", [P, L + LC])
                v = sb(st, "v", [P, NT + NC, P])
                E = [sb(st, f"E{i}", [P, 2 * L]) for i in range(2)]
                att = sb(st, "att", [P, L])
                kTc = sb(st, "kTc", [P, 4, P])
                kTf, kTb = sb(st, "kTf", [P, 3, P]), sb(st, "kTb", [P, 3, P])
                Sf, Sb = sb(st, "Sf", [P, NT, P]), sb(st, "Sb", [P, NT, P])
                cdec = sb(st, "cdec", [P, 2, NT])
                rq, rk = sb(st, "rq", [P, L]), sb(st, "rk", [P, L])
                rkc = sb(st, "rkc", [P, LC])
                rv = sb(st, "rv", [P, NT + NC, 2 * P])
                ratt = [sb(st, f"ratt{i}", [P, L]) for i in range(2)]
                strip = sb(st, "strip", [P, 7 * P])
                kw = sb(st, "kw", [P, 4, P])
                rS = sb(st, "rS", [P, 4, P])
                gate = [sb(st, f"gate{i}", [P, L]) for i in range(3)]
                y = [sb(st, n, [P, 3, L], F32R) for n in ("y_hi", "y_lo")]

                EXPS = {0: 0, 1: 1, 2: 2, 3: 3, 4: 4, 5: 5, 6: 6, 7: 7, 9: 8, 10: 9, 11: 10}
                ARGS = {0: 0, 1: 1, 2: 2, 3: 3, 4: 4, 5: 5, 6: 6, 7: 7, 9: 8, 10: 9}
                NJ = 12

                def of(h, k, n):
                    number, late, _ = h
                    return number * k + (n - k * late)

                def wait_full(eng, name, h):
                    eng.wait_ge(full[bank_of[name]], of(h, per[bank_of[name]], places[h[2]][name] + 1))

                def wait_free(pe, name, h, *copied):
                    need = {bank_of[name]: places[h[2]][name]}
                    for other in copied:
                        need[bank_of[other]] = max(need.get(bank_of[other], -99), places[h[2]][other] + 1)
                    for b, n in need.items():
                        after(pe, free[b], of(h, per[b], n))

                def wait_emptied(eng, name, h):
                    after(eng, free[bank_of[name]], of(h, per[bank_of[name]], places[h[2]][name] + 1))

                def over_heads(eng, work):
                    work(0, "first")
                    with eng.Fori(1, H) as h:
                        work(h, "loop")
                    work(H, "last")

                def head_of(i, phase, step):
                    return (i, int(step[-1] == "'"), phase)

                def halves(t, h):
                    return t.rearrange("p (b s h) -> p b s h", s=2, h=h)

                def chunks(t):
                    return t.rearrange("p (c t) -> p c t", t=P)

                with nc.Block() as block:
                    @block.sync
                    def _(sp):
                        w_pa, w_pb = (a[n].rearrange("a (k p) n -> p (a k) n", p=P) for n in ("w_proj_hgrn", "w_proj_ret"))

                        def loads(i, phase):
                            for name, n in slabs[phase].items():
                                if phase == "first" and n < 2:
                                    continue
                                s = i * NSLAB + n
                                if name in SLABS:
                                    col, step, tile, _ = SLABS[name]
                                    load_slab(sp, n % 2, w_in[:, :, bass.ds((i + (-1)) * step + (step + col + tile * P), P)], P, s)
                                elif name == "pa":
                                    load_slab(sp, n % 2, w_pa[:, bass.ds(i + (-1), 1), :], D, s)
                                else:
                                    half = int(name[2:])
                                    load_slab(sp, n % 2, w_pb[:, bass.ds(i * 2 + (-2), 2), half * 512:(half + 1) * 512], 512, s)
                                if name in MOD_AFTER:
                                    m = MOD_AFTER[name]
                                    tile = i * 4 + (16 + m)
                                    after(sp, mraw_used, i * 4 + m)
                                    sp.dma_start(mraw[:, :, :], wmod[:, :, bass.ds(tile * P, P)]).then_inc(mraw_in, 16)

                        over_heads(sp, loads)
                        for j in range(2):
                            load_slab(sp, j, w_in[:, :, COL["ga"] + j * P:COL["ga"] + (j + 1) * P], P, H * NSLAB + j)

                    @block.gpsimd
                    def _(pool):
                        def work(i, phase):
                            for name, n in slabs[phase].items():
                                if phase != "first" or n >= 2:
                                    split_lo(pool, i * NSLAB + n, n % 2)
                                if name in MOD_AFTER:
                                    pool.wait_ge(mraw_in, i * 64 + (16 * MOD_AFTER[name] + 16))
                                    pool.tensor_tensor(mraw[:, :, :], mraw[:, :, :], silu_c[:, 0:KT].unsqueeze(2).to_broadcast([P, KT, P]), ALU.mult)
                                    for k in (4, 2, 1):
                                        pool.drain()
                                        m = pool.tensor_tensor(mraw[:, 0:k, :], mraw[:, 0:k, :], mraw[:, k:2 * k, :], ALU.add)
                                    m.then_inc(mraw_summed, 1)

                        over_heads(pool, work)
                        for slot in range(2):
                            split_lo(pool, H * NSLAB + slot, slot)

                    @block.tensor
                    def _(pe):
                        def gemm(h, name, part):
                            s = slabs[h[2]][name]
                            slot = s % 2
                            if part == "a":
                                pe.wait_ge(lo_done, of(h, NSLAB, s + 3))
                                wait_free(pe, name, h)
                            if part == "c":
                                wait_free(pe, name + ".ctx", h)
                                for k in range(KT):
                                    m = passes(pe, at(name + ".ctx"), slot, k * P, hc, lambda t: t[:, k, :], k == 0, k == KT - 1)
                                m.then_inc(full[bank_of[name + ".ctx"]], 1)
                                return
                            for k in (range(KT // 2) if part == "a" else range(KT // 2, KT)):
                                m = passes(pe, at(name), slot, k * P, hx, lambda t: t[:, k, :], k == 0, k == KT - 1)
                            if part == "b":
                                m.then_inc(full[bank_of[name]], 1)

                        def transposes(h, name, src, n, *copied):
                            wait_free(pe, name, h, *copied)
                            for t in range(n):
                                m = pe.transpose(at(name)[:, t * P:(t + 1) * P], src(t), ident[:, :])
                            m.then_inc(full[bank_of[name]], 1)

                        def project(h, i, name, part, ys):
                            s = slabs[h[2]][name]
                            if part == "0":
                                pe.wait_ge(lo_done, i * NSLAB + (s + 3))
                            for n in tiles_of(name, part):
                                j = n - PROJ[name][0]
                                dst = f"{name[:2]}{n}"
                                wait_free(pe, dst, h)
                                for k, yt in enumerate(ys):
                                    m = passes(pe, at(dst), s % 2, k * 512 + j * P, y, lambda t: t[:, yt, :], k == 0, k == len(ys) - 1)
                                m.then_inc(full[bank_of[dst]], 1)

                        def head(pass_n, phase):
                            for step in PHASES[phase]:
                                h = head_of(pass_n, phase, step)
                                step = step.rstrip("'")
                                name, _, part = step.partition(".")
                                if name in SLABS and part in ("a", "b", "c"):
                                    gemm(h, name, part)
                                elif name.startswith("mod"):
                                    m_ = int(name[3:])
                                    pe.wait_ge(mraw_summed, of(h, 4, m_ + 1))
                                    wait_free(pe, name + ".ctx", h)
                                    pe.matmul(at(name + ".ctx")[:, 0:1], mraw[:, 0, :], ones[:, 0:1], start=True, stop=True)\
                                        .then_inc(full[bank_of[name + ".ctx"]], 1)
                                elif name in ("Tv", "Trv0", "Trv1"):
                                    transposes(h, name, lambda t: vT[:, t * P:(t + 1) * P], NT, name[1:], name[1:] + ".ctx")
                                    transposes(h, name + "c", lambda t: vT[:, L + t * P:L + (t + 1) * P], NC)
                                elif name == "job0":
                                    pe.wait_ge(mul_done, of(h, NJ, 1))
                                    transposes(h, "job0", lambda t: E[0][:, t * P:(t + 1) * P], 4)
                                elif name == "KVc":
                                    wait_free(pe, name, h, "job0", "Tv", "Tvc")
                                    for d in range(2):
                                        for c in range(NC):
                                            m = pe.matmul(at(name)[:, d * P:(d + 1) * P], kTc[:, NC * d + c, :], v[:, NT + c, :],
                                                          start=(c == 0), stop=(c == NC - 1))
                                    m.then_inc(full[bank_of[name]], 1)
                                elif name in ("job9", "job10"):
                                    j = int(name[3:])
                                    pe.wait_ge(mul_done, of(h, NJ, j + 1))
                                    order = [0, 1, 2] if j == 9 else [3, 2, 1]
                                    transposes(h, name, lambda t: E[j % 2][:, L + order[t] * P:L + (order[t] + 1) * P], 3)
                                elif name.startswith("job"):
                                    j = int(name[3:])
                                    pe.wait_ge(mul_done, of(h, NJ, j + 1))
                                    wait_free(pe, name, h)
                                    for c in range(NT):
                                        rhs = q[:, c * P:(c + 1) * P] if j == 8 else E[j % 2][:, c * P:(c + 1) * P]
                                        m = pe.matmul(at(name)[:, c * P:(c + 1) * P], E[j % 2][:, L + c * P:L + (c + 1) * P], rhs, start=True, stop=True)
                                    m.then_inc(full[bank_of[name]], 1)
                                elif name in ("KVf", "KVb"):
                                    f = name == "KVf"
                                    wait_free(pe, name, h, "job9" if f else "job10")
                                    for i, c in enumerate([0, 1, 2] if f else [3, 2, 1]):
                                        m = pe.matmul(at(name)[:, i * P:(i + 1) * P], (kTf if f else kTb)[:, i, :], v[:, c, :], start=True, stop=True)
                                    m.then_inc(full[bank_of[name]], 1)
                                elif name == "rkT":
                                    transposes(h, name, lambda t: rkc[:, t * P:(t + 1) * P], NC, "rk.ctx")
                                elif name == "rKV":
                                    wait_free(pe, name, h, "rkT", "Trv1", "Trv1c")
                                    for d in range(2):
                                        for c in range(NC):
                                            m = pe.matmul(at(name)[:, d * 256:(d + 1) * 256], kw[:, NC * d + c, :], rv[:, NT + c, :],
                                                          start=(c == 0), stop=(c == NC - 1))
                                    m.then_inc(full[bank_of[name]], 1)
                                elif name.startswith("att"):
                                    i = int(name[3:])
                                    if i == 0:
                                        pe.wait_ge(rk_ready, of(h, 1, 1))
                                        pe.wait_ge(rq_ready, of(h, 1, 1))
                                    wait_free(pe, name, h)
                                    pe.matmul(at(name), rk[:, i * P:(i + 1) * P], rq[:, :], start=True, stop=True).then_inc(full[bank_of[name]], 1)
                                elif name.startswith("av"):
                                    i = int(name[2:])
                                    if i == 0:
                                        wait_free(pe, "ro0", h)
                                        wait_free(pe, "ro1", h)
                                    wait_emptied(pe, f"att{i}", h)
                                    for e in range(2):
                                        m = pe.matmul(at(f"ro{e}"), rv[:, i, e * P:(e + 1) * P], ratt[i % 2][:, :], start=(i == 0), stop=False)
                                    m.then_inc(rav_done, 1)
                                elif name == "rstate":
                                    wait_emptied(pe, "rKV", h)
                                    pe.wait_ge(mul_done, of(h, NJ, 12))
                                    for e in range(2):
                                        for d in range(2):
                                            m = pe.matmul(at(f"ro{e}"), rS[:, 2 * d + e, :], E[1][:, d * L:(d + 1) * L], start=False, stop=(d == 1))
                                        m.then_inc(full[6 + e], 1)
                                elif name == "hgo":
                                    wait_free(pe, "ho", h, "job8", "KVf", "KVb")
                                    for c in range(NT):
                                        cs = slice(c * P, (c + 1) * P)
                                        pe.matmul(at("ho")[:, cs], v[:, c, :], att[:, cs], start=True, stop=False)
                                        pe.matmul(at("ho")[:, cs], Sf[:, c, :], bf[:, cs], start=False, stop=False)
                                        m = pe.matmul(at("ho")[:, cs], Sb[:, c, :], bb[:, cs], start=False, stop=True)
                                    m.then_inc(full[5], 1)
                                elif name == "hstat":
                                    pe.wait_ge(hsq_ready, of(h, 1, 1))
                                    wait_free(pe, name, h)
                                    pe.matmul(at(name), ones[:, 0:P], E[0][:, 0:L], start=True, stop=True).then_inc(full[bank_of[name]], 1)
                                elif name == "rmean":
                                    pe.wait_ge(rsum_ready, of(h, 2, 1))
                                    wait_free(pe, name, h)
                                    pe.matmul(at(name), ones[:, 0:P], att[:, :], start=True, stop=True).then_inc(full[bank_of[name]], 1)
                                elif name == "rvar":
                                    pe.wait_ge(rsum_ready, of(h, 2, 2))
                                    wait_free(pe, name, h)
                                    pe.matmul(at(name), ones[:, 0:P], rk[:, :], start=True, stop=True).then_inc(full[bank_of[name]], 1)
                                elif name == "pa":
                                    if part == "0":
                                        pe.wait_ge(hy_done, of(h, 1, 1))
                                    project(h, pass_n, name, part, [0])
                                elif name in ("pb0", "pb1"):
                                    if step == "pb0.0":
                                        pe.wait_ge(ry_done, of(h, 1, 1))
                                    project(h, pass_n, name, part, [1, 2])

                        over_heads(pe, head)

                    @block.scalar
                    def _(act):
                        def head(pass_n, phase):
                            for step in PHASES[phase]:
                                h = head_of(pass_n, phase, step)
                                step = step.rstrip("'")
                                name, _, part = step.partition(".")
                                if step in ("rg0.d", "rg1.d", "g.d"):
                                    i = ("rg0", "rg1", "g").index(name)
                                    wait_full(act, name, h)
                                    if phase != "first":
                                        act.wait_ge(hy_done if name == "g" else ry_done, of(h, 1, 0))
                                    act.activation(gate[i][:, :], at(name), ACT.Silu).then_inc(free[bank_of[name]], 1)
                                elif step in ("f.d", "b.d"):
                                    wait_full(act, name, h)
                                    act.activation((bf if name == "f" else bb)[:, :], at(name), ACT.Sigmoid)
                                    act.activation((kf if name == "f" else kb)[:, :], at(name), ACT.Sigmoid, scale=-1.0).then_inc(free[bank_of[name]], 1)
                                elif step in ("f.e", "b.e"):
                                    src = name + ".ctx"
                                    wait_full(act, src, h)
                                    act.activation((gfc if name == "f" else gbc)[:, :], at(src), ACT.Sigmoid)
                                    act.activation((kfc if name == "f" else kbc)[:, :], at(src), ACT.Sigmoid, scale=-1.0).then_inc(free[bank_of[src]], 1)
                                elif step == "gates":
                                    act.drain()
                                    act.wait_ge(hp_ready, of(h, 1, 1))
                                    for t, lb, om in ((gfc, LBF, OMF), (gbc, LBB, OMB), (bf, LBF, OMF), (bb, LBB, OMB)):
                                        m = act.activation(t[:, :], t[:, :], ACT.Ln, bias=hp[:, lb:lb + 1], scale=hp[:, om:om + 1])
                                    m.then_inc(ln_ready, 1)
                                elif step == "strip":
                                    act.wait_ge(strip_arg, of(h, 1, 1))
                                    act.activation(strip[:, :], strip[:, :], ACT.Exp).then_inc(strip_exp, 1)
                                elif step == "q.d":
                                    wait_full(act, name, h)
                                    act.activation(q[:, :], at(name), ACT.Copy, scale=QSCALE).then_inc(free[bank_of[name]], 1)
                                elif step in ("v.d", "rv0.d", "rv1.d"):
                                    wait_full(act, name, h)
                                    act.activation(vT[:, 0:L], at(name), ACT.Copy).then_inc(free[bank_of[name]], 1)
                                elif step in ("v.e", "rv0.e", "rv1.e"):
                                    wait_full(act, name + ".ctx", h)
                                    act.activation(vT[:, L:L + LC], at(name + ".ctx"), ACT.Copy).then_inc(free[bank_of[name + ".ctx"]], 1)
                                elif step == "rk.e":
                                    wait_full(act, "rk.ctx", h)
                                    act.activation(rkc[:, :], at("rk.ctx"), ACT.Copy).then_inc(free[bank_of["rk.ctx"]], 1)
                                elif step == "Tv":
                                    wait_full(act, "Tv", h)
                                    act.activation(v[:, 0:NT, :], chunks(at("Tv")), ACT.Copy).then_inc(free[bank_of["Tv"]], 1)
                                    wait_full(act, "Tvc", h)
                                    act.activation(v[:, NT:NT + NC, :], chunks(at("Tvc")[:, 0:LC]), ACT.Copy).then_inc(free[bank_of["Tvc"]], 1)
                                elif step in ("Trv0", "Trv1"):
                                    e = int(step[-1])
                                    wait_full(act, step, h)
                                    act.activation(rv[:, 0:NT, e * P:(e + 1) * P], chunks(at(step)), ACT.Copy).then_inc(free[bank_of[step]], 1)
                                    wait_full(act, step + "c", h)
                                    act.activation(rv[:, NT:NT + NC, e * P:(e + 1) * P], chunks(at(step + "c")[:, 0:LC]), ACT.Copy)\
                                        .then_inc(free[bank_of[step + "c"]], 1)
                                elif name.startswith("prep"):
                                    j = int(name[4:])
                                    e = E[j % 2]
                                    if j in ARGS:
                                        act.wait_ge(args_ready, of(h, len(ARGS), ARGS[j] + 1))
                                    if j == 0:
                                        act.activation(e[:, 0:L], e[:, 0:L], ACT.Exp).then_inc(exp_done, 1)
                                    elif 1 <= j <= 7:
                                        act.activation(e[:, :], e[:, :], ACT.Exp).then_inc(exp_done, 1)
                                    elif j in (9, 10):
                                        act.activation(e[:, 0:L], (bf if j == 9 else bb)[:, :], ACT.Exp)
                                        act.activation(e[:, L:2 * L], e[:, L:2 * L], ACT.Exp).then_inc(exp_done, 1)
                                    elif j == 11:
                                        wait_full(act, "job9", h)
                                        act.activation(e[:, 0:L], tpos[:, :], ACT.Exp, scale=hp[:, LGF:LGF + 1])
                                        act.activation(e[:, L:2 * L], tpos[:, ::-1], ACT.Exp, scale=hp[:, LGB:LGB + 1]).then_inc(exp_done, 1)
                                elif step in ("job0", "job9", "job10"):
                                    wait_full(act, step, h)
                                    dst, n = {"job0": (kTc, 4), "job9": (kTf, 3), "job10": (kTb, 3)}[step]
                                    act.activation(dst[:, :, :], chunks(at(step)[:, 0:n * P]), ACT.Copy).then_inc(free[bank_of[step]], 1)
                                elif step == "rkT":
                                    wait_full(act, step, h)
                                    for d in range(2):
                                        for c in range(NC):
                                            m = act.activation(kw[:, NC * d + c, :], at(step)[:, c * P:(c + 1) * P], ACT.Copy,
                                                               scale=hp[:, WC + NC * d + c:WC + NC * d + c + 1])
                                    m.then_inc(free[bank_of[step]], 1)
                                elif step == "rKV":
                                    wait_full(act, step, h)
                                    act.activation(rS[:, :, :], chunks(at(step)), ACT.Copy).then_inc(free[bank_of[step]], 1)
                                elif step == "hstat":
                                    wait_full(act, "ho", h)
                                    act.activation(E[0][:, 0:L], at("ho"), ACT.Square).then_inc(hsq_ready, 1)
                                elif step == "rmean":
                                    wait_full(act, "ro0", h)
                                    act.activation(ratt[0][:, :], at("ro0"), ACT.Copy).then_inc(free[6], 1)
                                    wait_full(act, "ro1", h)
                                    act.activation(ratt[1][:, :], at("ro1"), ACT.Copy).then_inc(free[7], 1)
                                elif step == "lns":
                                    wait_full(act, "hstat", h)
                                    act.activation(E[0][:, L:2 * L], at("hstat"), ACT.Ln, bias=eps[:, 0:1], scale=1.0 / P).then_inc(free[bank_of["hstat"]], 1)
                                    wait_full(act, "rvar", h)
                                    act.activation(rq[:, :], at("rvar"), ACT.Ln, bias=eps[:, 1:2], scale=1.0 / (2 * P)).then_inc(free[bank_of["rvar"]], 1)
                                elif step == "rcent":
                                    wait_emptied(act, "rmean", h)
                                    act.activation(rk[:, :], ratt[0][:, :], ACT.Square)
                                    act.activation(rq[:, :], ratt[1][:, :], ACT.Square).then_inc(rsq_ready, 1)
                                elif step == "norms":
                                    act.drain()
                                    act.activation(E[0][:, L:2 * L], E[0][:, L:2 * L], ACT.Exp, scale=-0.5).then_inc(hrs_ready, 1)
                                    act.activation(rq[:, :], rq[:, :], ACT.Exp, scale=-0.5).then_inc(rrs_ready, 1)
                                last = None
                                if name in PROJ:
                                    if tiles_of(name, part)[-1] != PROJ[name][-1]:
                                        continue
                                    last = f"{name[:2]}{PROJ[name][-1]}"
                                elif name in SLABS and part == ("e" if SLABS[name][3] else "d"):
                                    last = name + (".ctx" if part == "e" else "")
                                if last:
                                    s = slabs[phase][name] + 2
                                    wait_full(act, last, h)
                                    split_hi(act, pass_n * (NSLAB // 2) + s // 2, s % 2)

                        over_heads(act, head)

                    @block.vector
                    def _(dve):
                        def rope(h, name, dst, scale, ready):
                            tmp = ratt[0]
                            dve.drain()
                            wait_full(dve, name, h)
                            ps = at(name)
                            dve.scalar_tensor_tensor(out=dst[:, :], in0=ps, scalar=scale, in1=cosT[:, :], op0=ALU.mult, op1=ALU.mult)
                            dve.scalar_tensor_tensor(out=tmp[64:P, :], in0=ps[0:64, :], scalar=scale, in1=sinT[0:64, :], op0=ALU.mult, op1=ALU.mult)
                            dve.scalar_tensor_tensor(out=tmp[0:64, :], in0=ps[64:P, :], scalar=scale, in1=sinT[64:P, :], op0=ALU.mult,
                                                     op1=ALU.mult).then_inc(free[bank_of[name]], 1)
                            dve.drain()
                            dve.tensor_tensor(dst[:, :], dst[:, :], tmp[:, :], ALU.add).then_inc(ready, 1)

                        def accumulate(h, name, tiles, dst):
                            for n in tiles:
                                wait_full(dve, f"{name}{n}", h)
                                dve.tensor_tensor(dst[:, n, :], dst[:, n, :], at(f"{name}{n}"), ALU.add).then_inc(free[bank_of[f"{name}{n}"]], 1)

                        def head(pass_n, phase):
                            for step in PHASES[phase]:
                                h = head_of(pass_n, phase, step)
                                step = step.rstrip("'")
                                name, _, part = step.partition(".")
                                if name.startswith("mod"):
                                    wait_full(dve, name + ".ctx", h)
                                    dve.nop().then_inc(mraw_used, 1)
                                    m_ = int(name[3:])
                                    dve.tensor_copy(modt[:, bass.ds(pass_n * 4 + (16 + m_), 1), 0:1].rearrange("p a n -> p (a n)"),
                                                    at(name + ".ctx")[:, 0:1]).then_inc(free[bank_of[name + ".ctx"]], 1)
                                elif step == "gates":
                                    dve.wait_ge(ln_ready, of(h, 1, 1))
                                    e = E[0]
                                    dve.memset(e[:, LC - 1:LC + 1], 0.0)
                                    dve.tensor_tensor_scan(e[:, LC - 2::-1], ones[:, 0:LC - 1], gfc[:, LC - 1:0:-1], 0.0, ALU.mult, ALU.add)
                                    dve.tensor_tensor_scan(e[:, LC + 1:2 * LC], ones[:, 0:LC - 1], gbc[:, 0:LC - 1], 0.0, ALU.mult, ALU.add)\
                                        .then_inc(args_ready, 1)
                                    for t, om in ((kfc, OMF), (kbc, OMB), (kf, OMF), (kb, OMB)):
                                        dve.tensor_scalar(t[:, :], t[:, :], hp[:, om:om + 1], None, ALU.mult)
                                    dve.tensor_tensor_scan(bf[:, :], first[:, :], bf[:, :], 0.0, ALU.mult, ALU.add)
                                    dve.tensor_tensor_scan(bb[:, ::-1], first[:, :], bb[:, ::-1], 0.0, ALU.mult, ALU.add)
                                    dve.drain()
                                elif step == "strip":
                                    dve.tensor_scalar(strip[:, :], upos[:, :], hp[:, LGF:LGF + 1], None, ALU.mult)
                                    dve.drain()
                                    dve.scalar_tensor_tensor(out=strip[:, :], in0=uneg[:, :], scalar=hp[:, LGB:LGB + 1], in1=strip[:, :],
                                                             op0=ALU.mult, op1=ALU.add).then_inc(strip_arg, 1)
                                elif name.startswith("prep"):
                                    j = int(name[4:])
                                    e = E[j % 2]
                                    if 1 <= j <= 7:
                                        if j >= 2:
                                            wait_full(dve, f"job{j - 2}", h)
                                        hh = HALVES[j - 1]
                                        nb = L // (2 * hh)
                                        eq, ek = halves(e[:, 0:L], hh), halves(e[:, L:2 * L], hh)
                                        f_, b_ = halves(bf[:, :], hh), halves(bb[:, :], hh)
                                        fm = f_[:, :, 0, hh - 1:hh].to_broadcast([P, nb, hh])
                                        bm = b_[:, :, 1, 0:1].to_broadcast([P, nb, hh])
                                        dve.tensor_tensor(eq[:, :, 1, :], f_[:, :, 1, :], fm, ALU.subtract)
                                        dve.tensor_tensor(eq[:, :, 0, :], b_[:, :, 0, :], bm, ALU.subtract)
                                        dve.tensor_tensor(ek[:, :, 0, :], fm, f_[:, :, 0, :], ALU.subtract)
                                        dve.tensor_tensor(ek[:, :, 1, :], bm, b_[:, :, 1, :], ALU.subtract).then_inc(args_ready, 1)
                                    elif j in (9, 10):
                                        wait_full(dve, f"job{j - 2}", h)
                                        src = chunks((bf if j == 9 else bb)[:, :])
                                        edge = src[:, :, P - 1:P] if j == 9 else src[:, :, 0:1]
                                        dve.tensor_tensor(chunks(e[:, L:2 * L]), edge.to_broadcast([P, NT, P]), src, ALU.subtract).then_inc(args_ready, 1)
                                elif name.startswith("mul"):
                                    j = int(name[3:])
                                    e = E[j % 2]
                                    if j in EXPS:
                                        dve.wait_ge(exp_done, of(h, len(EXPS), EXPS[j] + 1))
                                    if j == 0:
                                        dve.tensor_tensor(e[:, 0:LC], e[:, 0:LC], kfc[:, :], ALU.mult)
                                        dve.tensor_tensor(e[:, LC:2 * LC], e[:, LC:2 * LC], kbc[:, :], ALU.mult).then_inc(mul_done, 1)
                                    elif 1 <= j <= 7:
                                        hh = HALVES[j - 1]
                                        ek, f_, b_ = halves(e[:, L:2 * L], hh), halves(kf[:, :], hh), halves(kb[:, :], hh)
                                        if j == 1:
                                            wait_emptied(dve, "q", h)
                                        dve.tensor_tensor(e[:, 0:L], e[:, 0:L], q[:, :], ALU.mult)
                                        dve.tensor_tensor(ek[:, :, 0, :], ek[:, :, 0, :], f_[:, :, 0, :], ALU.mult)
                                        dve.tensor_tensor(ek[:, :, 1, :], ek[:, :, 1, :], b_[:, :, 1, :], ALU.mult).then_inc(mul_done, 1)
                                    elif j == 8:
                                        wait_full(dve, "job6", h)
                                        dve.tensor_tensor(e[:, L:2 * L], kf[:, :], kb[:, :], ALU.add).then_inc(mul_done, 1)
                                    elif j in (9, 10):
                                        k_, s_ = (kf, bf) if j == 9 else (kb, bb)
                                        d = j - 9
                                        eq = chunks(e[:, 0:L])
                                        dve.tensor_copy(cdec[:, d, :].unsqueeze(2), eq[:, :, P - 1:P] if d == 0 else eq[:, :, 0:1])
                                        dve.tensor_tensor(s_[:, :], e[:, 0:L], q[:, :], ALU.mult)
                                        dve.tensor_tensor(e[:, L:2 * L], e[:, L:2 * L], k_[:, :], ALU.mult).then_inc(mul_done, 1)
                                    elif j == 11:
                                        dve.tensor_tensor(e[:, 0:L], e[:, 0:L], rq[:, :], ALU.mult)
                                        dve.tensor_tensor(e[:, L:2 * L], e[:, L:2 * L], rq[:, :], ALU.mult).then_inc(mul_done, 1)
                                elif name.startswith("post"):
                                    j = int(name[4:])
                                    if j > 1:
                                        dve.drain()
                                    if j == 1:
                                        dve.tensor_copy(att[:, :], at("job1")).then_inc(free[bank_of["job1"]], 1)
                                    else:
                                        mask = masks[:, (j - 1) * P:j * P].unsqueeze(1).to_broadcast([P, NT, P])
                                        dve.copy_predicated(chunks(att[:, :]), mask, chunks(at(f"job{j}"))).then_inc(free[bank_of[f"job{j}"]], 1)
                                elif step == "rk.d":
                                    rope(h, "rk", rk, 1.0, rk_ready)
                                elif step == "rq.d":
                                    rope(h, "rq", rq, QSCALE, rq_ready)
                                elif step == "KVc":
                                    wait_full(dve, step, h)
                                    dve.tensor_copy(Sf[:, 0, :], at(step)[:, 0:P])
                                    dve.tensor_copy(Sb[:, NT - 1, :], at(step)[:, P:2 * P]).then_inc(free[bank_of[step]], 1)
                                elif step in ("KVf", "KVb"):
                                    f = step == "KVf"
                                    S, d = (Sf, 0) if f else (Sb, 1)
                                    for i in range(3):
                                        c, n = (i, i + 1) if f else (3 - i, 2 - i)
                                        dve.drain()
                                        if i == 0:
                                            wait_full(dve, step, h)
                                        m = dve.scalar_tensor_tensor(out=S[:, n, :], in0=S[:, c, :], scalar=cdec[:, d, c:c + 1],
                                                                     in1=at(step)[:, i * P:(i + 1) * P], op0=ALU.mult, op1=ALU.add)
                                    m.then_inc(free[bank_of[step]], 1)
                                elif name.startswith("att"):
                                    i = int(name[3:])
                                    wait_full(dve, name, h)
                                    if i == 0:
                                        dve.wait_ge(strip_exp, of(h, 1, 1))
                                        dve.tensor_tensor(strip[:, 3 * P:4 * P], strip[:, 3 * P:4 * P], ident[:, :], ALU.add)
                                        dve.drain()
                                    if i >= 2:
                                        dve.wait_ge(rav_done, of(h, 4, i - 1))
                                    o = (3 - i) * P
                                    dve.tensor_tensor(ratt[i % 2][:, :], at(name), strip[:, o:o + L], ALU.mult).then_inc(free[bank_of[name]], 1)
                                elif step == "rmean":
                                    wait_emptied(dve, "ro0", h)
                                    wait_emptied(dve, "ro1", h)
                                    dve.tensor_tensor(att[:, :], ratt[0][:, :], ratt[1][:, :], ALU.add).then_inc(rsum_ready, 1)
                                elif step == "rvar":
                                    dve.wait_ge(rsq_ready, of(h, 1, 1))
                                    dve.tensor_tensor(rk[:, :], rk[:, :], rq[:, :], ALU.add).then_inc(rsum_ready, 1)
                                elif step == "rcent":
                                    wait_full(dve, "rmean", h)
                                    for e in range(2):
                                        m = dve.scalar_tensor_tensor(out=ratt[e][:, :], in0=at("rmean"), scalar=-1.0 / (2 * P), in1=ratt[e][:, :],
                                                                     op0=ALU.mult, op1=ALU.add)
                                    m.then_inc(free[bank_of["rmean"]], 1)
                                elif step == "norms":
                                    hn = E[0][:, L:2 * L]
                                    dve.wait_ge(hrs_ready, of(h, 1, 1))
                                    dve.tensor_tensor(hn, at("ho"), hn, ALU.mult).then_inc(free[5], 1)
                                    dve.drain()
                                    dve.scalar_tensor_tensor(out=hn, in0=hn, scalar=hgn[:, 0:1], in1=gate[2][:, :], op0=ALU.mult, op1=ALU.mult)
                                    dve.drain()
                                    dve.tensor_copy(y[0][:, 0, :], hn)
                                    dve.drain()
                                    dve.tensor_tensor(y[1][:, 0, :], hn, y[0][:, 0, :].bitcast(F32), ALU.subtract).then_inc(hy_done, 1)
                                    dve.wait_ge(rrs_ready, of(h, 1, 1))
                                    for e in range(2):
                                        dve.tensor_tensor(ratt[e][:, :], ratt[e][:, :], rq[:, :], ALU.mult)
                                    dve.drain()
                                    for e in range(2):
                                        dve.tensor_tensor(ratt[e][:, :], ratt[e][:, :], gate[e][:, :], ALU.mult)
                                    dve.drain()
                                    for e in range(2):
                                        dve.tensor_copy(y[0][:, 1 + e, :], ratt[e][:, :])
                                    dve.drain()
                                    for e in range(2):
                                        m = dve.tensor_tensor(y[1][:, 1 + e, :], ratt[e][:, :], y[0][:, 1 + e, :].bitcast(F32), ALU.subtract)
                                    m.then_inc(ry_done, 1)
                                elif name in PROJ:
                                    accumulate(h, name[:2], tiles_of(name, part), acc[0] if name == "pa" else acc[1])
                                elif step == "hgn":
                                    dve.tensor_copy(hgn[:, :], heads[:, bass.ds(pass_n + (-1), 1), HGN:HGN + 1].rearrange("p a n -> p (a n)"))
                                elif step == "hp":
                                    dve.tensor_copy(hp[:, :], heads[:, bass.ds(pass_n, 1), :].rearrange("p a n -> p (a n)")).then_inc(hp_ready, 1)

                        over_heads(dve, head)

        tail = top
        full, free = tail_full, tail_free
        x1 = sb(tail, "x1", [P, KT, L])
        sqsum, sq, sc2 = sb(tail, "sqsum", [P, L]), sb(tail, "sq", [P, L]), sb(tail, "sc2", [P, KT])
        nt = [sb(tail, f"nt{i}", [P, L]) for i in range(2)]
        nu = [sb(tail, f"nu{i}", [P, L]) for i in range(2)]
        sqs = nt + nu
        OUT_BANK = ((1, 2, 3, 4), (5, 6, 7, 0))
        outs = [[acc[half][:, t, :] for t in range(NT)] for half in range(2)]
        sg = nn = nt + nu
        with ExitStack() as st:
            mrg = [sb(st, n, [P, KT, L], F32R) for n in ("mrg_hi", "mrg_lo")]
            xt2 = sb(st, "xt2", [P, NT, D])
        g = [sb(tail, n, [P, FT, L], F32R) for n in ("g_hi", "g_lo")]

        S0, HALF0 = H * NSLAB, H * NSLAB // 2
        SW = S0 + 2 * KT
        SF = SW + KT
        SD = SF + 2 * FT
        BEFORE_DOWN = [4 + FT // 2] * 4 + [6, 6, 3, 2]

        def product(pe, b, n_before, s, slot, pair, made=None):
            pe.wait_ge(lo_done, s + 3)
            after(pe, free[b], n_before)
            for k in range(KT):
                if made is not None:
                    pe.wait_ge(made, k + 1)
                m = passes(pe, bank(b), slot, k * P, pair, lambda t: t[:, k, :], k == 0, k == KT - 1)
            m.then_inc(full[b], 1)

        def one(t, n):
            return t[:, bass.ds(n, 1), :].rearrange("p a n -> p (a n)")

        with nc.Block() as block:
            @block.sync
            def _(sp):
                sp.dma_start(xt2[:, :, :], x_dram).then_inc(xt2_in, 16)
                w_out, w_gate, w_up, w_down = (a[n].rearrange("a (k p) n -> p (a k) n", p=P)
                                               for n in ("w_out", "w_ffn_gate", "w_ffn_up", "w_ffn_down"))

                def gate_slab(i, j):
                    col = (COL["ga"] if j < 2 else COL["gb"]) + (j % 2) * P
                    cols = slice(col, col + P) if isinstance(i, int) else bass.ds(i * (2 * P) + col, P)
                    load_slab(sp, j % 2, w_in[:, :, cols], P, i * 4 + (S0 + j))

                for j in (2, 3):
                    gate_slab(0, j)
                with sp.Fori(1, 4) as i:
                    for j in range(4):
                        gate_slab(i, j)
                with sp.Fori(0, 4) as i:
                    for j in range(2):
                        load_slab(sp, j, w_out[:, :, bass.ds(i * (2 * P) + j * P, P)], P, i * 2 + (SW + j))
                with sp.Fori(0, FT // 2) as i:
                    for j in range(4):
                        load_slab(sp, j % 2, (w_up if j % 2 else w_gate)[:, :, bass.ds(i * (2 * P) + (j // 2) * P, P)], P, i * 4 + (SF + j))
                with sp.Fori(0, FT // 2) as i:
                    for j in range(2):
                        load_slab(sp, j, w_down[:, bass.ds(i * 2 + j, 1), :], D, i * 2 + (SD + j))
                for half, t, copied, n in [(0, t, 0, t + 1) for t in range(NT)] + [(1, 0, 1, 1), (1, 1, 0, NT + 1), (1, 2, 1, 2), (1, 3, 0, NT + 2)]:
                    sp.wait_ge(y_copied[copied], n)
                    sp.dma_start(out[0, t * P:(t + 1) * P, half * 512:(half + 1) * 512], outs[half][t]).then_inc(y_stored, 16)
                sp.wait_ge(y_stored, 16 * 2 * NT)

            @block.gpsimd
            def _(pool):
                with pool.Fori(0, (SD + FT - S0 - 2) // 2) as i:
                    for slot in range(2):
                        split_lo(pool, i * 2 + (S0 + 2 + slot), slot)

            @block.tensor
            def _(pe):
                with pe.Fori(0, 4) as i:
                    for j in range(4):
                        product(pe, j, i, i * 4 + (S0 + j), j % 2, hx)
                pe.wait_ge(xt2_in, 16)
                for k in range(KT):
                    b = 4 + k % 4
                    if k >= 4:
                        after(pe, free[b], 1)
                    for t in range(NT):
                        m = pe.transpose(bank(b)[:, t * P:(t + 1) * P], xt2[:, t, k * P:(k + 1) * P], ident[:, :])
                    m.then_inc(full[b], 1)
                after(pe, mrg_done, KT)
                with pe.Fori(0, 4) as i:
                    for j in range(2):
                        product(pe, 4 + j, i + 2, i * 2 + (SW + j), j, mrg)
                after(pe, sqsum_done, KT)
                after(pe, free[6], 2)
                pe.matmul(bank(6), ones[:, 0:P], sqsum[:, :], start=True, stop=True).then_inc(full[6], 1)
                for j in range(4):
                    product(pe, j, 4, SF + j, j % 2, hx, hx2_ready if j == 0 else None)
                with pe.Fori(1, FT // 2) as i:
                    for j in range(4):
                        product(pe, j, i + 4, i * 4 + (SF + j), j % 2, hx)

                def down(k, slot, first_, last):
                    pe.wait_ge(lo_done, k + (SD + 3))
                    after(pe, g_done, k + 1)
                    for n in range(KT):
                        if first_:
                            after(pe, free[n], BEFORE_DOWN[n])
                        m = passes(pe, bank(n), slot, n * P, g, lambda t: t[:, k, :] if isinstance(k, int) else one(t, k), first_, last)
                        if last:
                            m.then_inc(full[n], 1)
                    if not last:
                        m.then_inc(down_used, 1)

                for k in range(2):
                    down(k, k, k == 0, False)
                with pe.Fori(1, FT // 2 - 1) as i:
                    for j in range(2):
                        down(i * 2 + j, j, False, False)
                for k in range(FT - 2, FT):
                    down(k, k % 2, False, k == FT - 1)
                after(pe, free[0], BEFORE_DOWN[0] + 1)
                for n in range(KT):
                    pe.wait_ge(sq_ready, KT + n + 1)
                    m = pe.matmul(bank(0), ones[:, 0:P], sqs[n % 4][:, :], start=(n == 0), stop=(n == KT - 1))
                    m.then_inc(sq_summed, 1)
                for half in range(2):
                    pe.wait_ge(fin_ready, 4 * (half + 1))
                    for t in range(NT):
                        b = OUT_BANK[half][t]
                        after(pe, free[b], BEFORE_DOWN[b] + (2 if b == 0 else 1))
                        for k in range(4):
                            m = pe.transpose(bank(b)[:, k * P:(k + 1) * P], x1[:, 4 * half + k, t * P:(t + 1) * P], ident[:, :])
                        m.then_inc(full[b], 1)

            @block.scalar
            def _(act):
                with act.Fori(0, 4) as i:
                    for j in range(4):
                        act.wait_ge(full[j], i + 1)
                        if j % 2 == 0:
                            after(act, mrg_done, i * 2)
                        act.activation(sg[j][:, :], bank(j), ACT.Sigmoid).then_inc(free[j], 1)
                        split_hi(act, i * 2 + (HALF0 + j // 2 + 1), j % 2)
                for k in range(KT):
                    b = 4 + k % 4
                    act.wait_ge(full[b], k // 4 + 1)
                    act.activation(x1[:, k, :], bank(b), ACT.Copy).then_inc(free[b], 1)
                with act.Fori(0, 4) as i:
                    for j in range(2):
                        act.wait_ge(full[4 + j], i + 3)
                        split_hi(act, i + (HALF0 + 9), j)
                        after(act, free[4 + j], i + 3)
                        after(act, sqsum_done, i * 2 + j)
                        act.activation(sq[:, :], one(x1, i * 2 + j), ACT.Square).then_inc(sq_ready, 1)

                def rstd(b, n):
                    if n is not None:
                        act.wait_ge(full[b], n)
                    act.activation(sqsum[:, :], bank(b), ACT.Ln, bias=eps[:, 0:1], scale=1.0 / D).then_inc(free[b], 1)
                    act.drain()
                    act.activation(sqsum[:, :], sqsum[:, :], ACT.Exp, scale=-0.5).then_inc(tail_rstd, 1)

                rstd(6, 3)
                act.wait_ge(mod_ready, 1)
                for k in range(KT):
                    act.wait_ge(nt_ready, k + 1)
                    act.activation(hx[0][:, k, :], nn[k % 4][:, :], ACT.Identity, bias=modt[:, 24 + k, 0:1]).then_inc(nu_ready, 1)
                with act.Fori(0, FT // 2) as i:
                    for j in range(4):
                        act.wait_ge(full[j], i + 5)
                        if j % 2 == 0:
                            after(act, g_done, i * 2)
                            act.wait_ge(hx2_ready, KT)
                            act.activation(nt[j // 2][:, :], bank(j), ACT.Silu).then_inc(free[j], 1)
                        split_hi(act, i * 2 + (HALF0 + 12 + j // 2 + 1), j % 2)
                with act.Fori(0, FT // 2 - 1) as i:
                    for j in range(2):
                        act.wait_ge(down_used, i * 2 + (j + 1))
                        split_hi(act, i + (HALF0 + 12 + FT + 1), j)
                for n in range(KT):
                    after(act, free[n], BEFORE_DOWN[n] + 1)
                    if n >= 4:
                        act.wait_ge(sq_summed, n - 3)
                    act.activation(sqs[n % 4][:, :], x1[:, n, :], ACT.Square).then_inc(sq_ready, 1)
                act.wait_ge(sq_summed, KT)
                rstd(0, None)
                for t in range(NT):
                    act.wait_ge(full[OUT_BANK[0][t]], BEFORE_DOWN[OUT_BANK[0][t]] + 2)
                    act.activation(outs[0][t], bank(OUT_BANK[0][t]), ACT.Copy).then_inc(y_copied[0], 1)
                for t in (1, 3):
                    act.wait_ge(full[OUT_BANK[1][t]], BEFORE_DOWN[OUT_BANK[1][t]] + 2)
                    act.activation(outs[1][t], bank(OUT_BANK[1][t]), ACT.Copy).then_inc(y_copied[0], 1)

            @block.vector
            def _(dve):
                dve.tensor_tensor(modt[:, 16:48, 0], modt[:, 16:48, 0], chan[:, PBM + 16:PBM + 48], ALU.add)
                dve.drain()
                dve.scalar_tensor_tensor(out=sc2[:, :], in0=modt[:, 32:40, 0], scalar=1.0, in1=chan[:, PN2:PN2 + 8],
                                         op0=ALU.add, op1=ALU.mult).then_inc(mod_ready, 1)
                dve.memset(sqsum[:, :], 0.0)
                with dve.Fori(0, 4) as i:
                    for j in range(2):
                        n = i * 2 + j
                        after(dve, free[j], i + 1)
                        dve.tensor_tensor(sg[j][:, :], sg[j][:, :], one(acc[0], n), ALU.mult)
                        after(dve, free[2 + j], i + 1)
                        dve.tensor_tensor(sg[2 + j][:, :], sg[2 + j][:, :], one(acc[1], n), ALU.mult)
                        dve.drain()
                        dve.tensor_tensor(sg[j][:, :], sg[j][:, :], sg[2 + j][:, :], ALU.add)
                        dve.drain()
                        dve.tensor_copy(one(mrg[0], n), sg[j][:, :])
                        dve.drain()
                        dve.tensor_tensor(one(mrg[1], n), sg[j][:, :], one(mrg[0], n).bitcast(F32), ALU.subtract).then_inc(mrg_done, 1)
                after(dve, free[7], 2)
                with dve.Fori(0, 4) as i:
                    for j in range(2):
                        n = i * 2 + j
                        dve.wait_ge(full[4 + j], i + 3)
                        g1 = modt[:, bass.ds(i * 2 + (16 + j), 1), 0:1].rearrange("p a c -> p (a c)")
                        dve.scalar_tensor_tensor(out=one(x1, n), in0=bank(4 + j), scalar=g1, in1=one(x1, n),
                                                 op0=ALU.mult, op1=ALU.add).then_inc(free[4 + j], 1)
                        dve.wait_ge(sq_ready, i * 2 + (j + 1))
                        dve.tensor_tensor(sqsum[:, :], sqsum[:, :], sq[:, :], ALU.add).then_inc(sqsum_done, 1)
                dve.wait_ge(tail_rstd, 1)

                def split_hx(k):
                    dve.wait_ge(nu_ready, k + 1)
                    dve.scalar_tensor_tensor(out=hx[1][:, k, :], in0=nn[k % 4][:, :], scalar=modt[:, 24 + k, 0:1], in1=hx[0][:, k, :].bitcast(F32),
                                             op0=ALU.add, op1=ALU.subtract).then_inc(hx2_ready, 1)

                for k in range(KT):
                    dve.scalar_tensor_tensor(out=nn[k % 4][:, :], in0=x1[:, k, :], scalar=sc2[:, k:k + 1], in1=sqsum[:, :],
                                             op0=ALU.mult, op1=ALU.mult).then_inc(nt_ready, 1)
                    if k >= 1:
                        split_hx(k - 1)
                split_hx(KT - 1)
                with dve.Fori(0, FT // 2) as i:
                    for t in range(2):
                        n = i * 2 + t
                        after(dve, free[2 * t], i + 5)
                        dve.wait_ge(full[2 * t + 1], i + 5)
                        dve.tensor_tensor(nu[t][:, :], bank(2 * t + 1), nt[t][:, :], ALU.mult).then_inc(free[2 * t + 1], 1)
                        dve.drain()
                        dve.tensor_copy(one(g[0], n), nu[t][:, :])
                        dve.drain()
                        dve.tensor_tensor(one(g[1], n), nu[t][:, :], one(g[0], n).bitcast(F32), ALU.subtract).then_inc(g_done, 1)
                for n in range(KT):
                    dve.wait_ge(full[n], BEFORE_DOWN[n] + 1)
                    dve.scalar_tensor_tensor(out=x1[:, n, :], in0=bank(n), scalar=modt[:, 40 + n, 0:1], in1=x1[:, n, :],
                                             op0=ALU.mult, op1=ALU.add).then_inc(free[n], 1)
                dve.wait_ge(tail_rstd, 2)
                for n in range(KT):
                    dve.scalar_tensor_tensor(out=x1[:, n, :], in0=x1[:, n, :], scalar=chan[:, PFN + n:PFN + n + 1], in1=sqsum[:, :],
                                             op0=ALU.mult, op1=ALU.mult).then_inc(fin_ready, 1)
                for t in (0, 2):
                    b = OUT_BANK[1][t]
                    dve.wait_ge(full[b], BEFORE_DOWN[b] + 2)
                    dve.tensor_copy(outs[1][t], bank(b)).then_inc(y_copied[1], 1)


_INS = ["x", "c", "ctx", "c_ctx", "w_mod", "b_mod", "norm1_w", "norm2_w", "w_in", "hg_lb_fwd", "hg_lb_bwd", "hg_norm_w",
        "rt_theta_fwd", "rt_theta_bwd", "w_proj_hgrn", "w_proj_ret", "w_out", "w_ffn_gate", "w_ffn_up", "w_ffn_down", "final_norm_w"]


def kernel(**inputs):
    import numpy as _np
    import concourse.bacc as _bacc
    from concourse import mybir as _mybir
    from concourse.bass_utils import run_bass_kernel_spmd as _run

    nc = _bacc.Bacc("TRN2", target_bir_lowering=False, num_devices=1)
    arrays, aps = {}, {}
    host = {n: _np.ascontiguousarray(inputs[n]) for n in _INS}
    host.update(constants())
    for name, arr in host.items():
        arrays[f"in_{name}_dram"] = arr
        aps[name] = nc.dram_tensor(f"in_{name}_dram", arr.shape, _mybir.dt.from_np(arr.dtype), kind="ExternalInput").ap()
    out = nc.dram_tensor("out_0_dram", (1, L, D), F32, kind="ExternalOutput").ap()
    build(nc, aps, out)
    r = _run(nc, [arrays], core_ids=[0])
    return r.results[0]["out_0_dram"]
```
